# Optimizing a Trainium2 kernel written in Bass

```python
import math
import jax, jax.numpy as jnp
from jax import lax
import numpy as np

D_MODEL = 1024
BATCH = 1
SEQ = 256
DEPTH = 1

PLE_DIM = 256
HEAD_DIM = 64
D_MIX = D_MODEL
SB_HEADS = D_MIX // 2 // HEAD_DIM
RET_HEADS = D_MIX // 2 // HEAD_DIM
SB_WIDTH = SB_HEADS * HEAD_DIM
RET_WIDTH = RET_HEADS * HEAD_DIM
D_IN = 3 * SB_WIDTH + 4 * RET_WIDTH
Q_BLOCK = 128
RET_CHUNK = 128
ROPE_BASE = 10000.0
N_EXPERTS = 32
TOP_K = 4
D_EXPERT = D_MODEL
SWIGLU_LIMIT = 7.0
SWIGLU_ALPHA = 1.702
MOE_BLOCK = 128
EPS = 1e-6


def _rmsnorm(x, g):
    xf = x.astype(jnp.float32)
    y = xf * lax.rsqrt(jnp.mean(xf * xf, axis=-1, keepdims=True) + EPS)
    return (y * g.astype(jnp.float32)).astype(x.dtype)

def _heads(t, n_heads):
    b, s, _ = t.shape
    return t.reshape(b, s, n_heads, HEAD_DIM).transpose(0, 2, 1, 3)

def _rope(t, positions):
    half = HEAD_DIM // 2
    inv_freq = ROPE_BASE ** (-jnp.arange(half, dtype=jnp.float32) / half)
    ang = positions.astype(jnp.float32)[:, None, :, None] * inv_freq
    cos, sin = jnp.cos(ang), jnp.sin(ang)
    tf = t.astype(jnp.float32)
    t1, t2 = tf[..., :half], tf[..., half:]
    return jnp.concatenate([t1 * cos - t2 * sin, t2 * cos + t1 * sin], axis=-1).astype(t.dtype)

def _stick_breaking(q, k, v):
    b, h, s, d = q.shape
    nqb = s // Q_BLOCK
    scale = 1.0 / math.sqrt(d)
    qs = q.reshape(b, h, nqb, Q_BLOCK, d).transpose(2, 0, 1, 3, 4)
    t0s = jnp.arange(nqb, dtype=jnp.int32) * Q_BLOCK
    kpos = jnp.arange(s, dtype=jnp.int32)

    def block(args):
        qb, t0 = args
        z = jnp.einsum('bhqd,bhkd->bhqk', qb, k).astype(jnp.float32) * scale
        qpos = t0 + jnp.arange(Q_BLOCK, dtype=jnp.int32)
        mask = kpos[None, :] < qpos[:, None]
        lneg = jnp.where(mask, jax.nn.log_sigmoid(-z), 0.0)
        tail = lax.cumsum(lneg, axis=3, reverse=True) - lneg
        w = jnp.where(mask, jnp.exp(jax.nn.log_sigmoid(z) + tail), 0.0)
        return jnp.einsum('bhqk,bhkd->bhqd', w.astype(v.dtype), v)

    out = lax.map(block, (qs, t0s))
    return out.transpose(1, 2, 0, 3, 4).reshape(b, h, s, d)

def _retention(q, k, v):
    b, h, s, d = q.shape
    n = s // RET_CHUNK
    c = RET_CHUNK
    log_g = jnp.log(1.0 - 2.0 ** (-5.0 - jnp.arange(h, dtype=jnp.float32)))
    idx = jnp.arange(c, dtype=jnp.float32)
    diff = idx[:, None] - idx[None, :]
    dmat = jnp.where(diff >= 0, jnp.exp(log_g[:, None, None] * jnp.maximum(diff, 0.0)), 0.0)
    k_dec = jnp.exp(log_g[:, None] * (c - 1 - idx)[None, :])
    q_dec = jnp.exp(log_g[:, None] * (idx + 1.0)[None, :])
    g_chunk = jnp.exp(log_g * c)
    qc = q.reshape(b, h, n, c, d)
    kc = k.reshape(b, h, n, c, d)
    vc = v.reshape(b, h, n, c, d)
    dt = q.dtype
    scores = jnp.einsum('bhnid,bhnjd->bhnij', qc, kc) * dmat[None, :, None].astype(dt)
    inner = jnp.einsum('bhnij,bhnjd->bhnid', scores, vc)
    kv = jnp.einsum('bhnjd,bhnje->bhnde', kc * k_dec[None, :, None, :, None].astype(dt), vc)

    def step(state, kv_n):
        return g_chunk[:, None, None].astype(state.dtype) * state + kv_n, state

    init = jnp.zeros((b, h, d, d), dtype=kv.dtype)
    _, prev = lax.scan(step, init, jnp.moveaxis(kv, 2, 0))
    prev = jnp.moveaxis(prev, 0, 2)
    cross = jnp.einsum('bhnid,bhnde->bhnie', qc, prev) * q_dec[None, :, None, :, None].astype(dt)
    return (inner + cross).reshape(b, h, s, d)

def _group_norm(y, gain, bias):
    yf = y.astype(jnp.float32)
    mu = jnp.mean(yf, axis=-1, keepdims=True)
    var = jnp.mean((yf - mu) ** 2, axis=-1, keepdims=True)
    yn = (yf - mu) * lax.rsqrt(var + EPS)
    b, h, s, d = y.shape
    yn = yn.transpose(0, 2, 1, 3).reshape(b, s, h * d)
    return (yn * gain.astype(jnp.float32) + bias.astype(jnp.float32)).astype(y.dtype)

def _moe(xt, w_router, b_router, w_up_gate, b_up_gate, w_down, b_down):
    t, d = xt.shape
    logits = (xt @ w_router + b_router).astype(jnp.float32)
    top_vals, top_idx = lax.top_k(logits, TOP_K)
    gates = jax.nn.softmax(top_vals, axis=-1)
    a = t * TOP_K
    flat_e = top_idx.reshape(a).astype(jnp.int32)
    flat_tok = jnp.arange(a, dtype=jnp.int32) // TOP_K
    flat_gate = gates.reshape(a)
    order = jnp.argsort(flat_e)
    sorted_e = flat_e[order]
    counts = jnp.zeros((N_EXPERTS,), jnp.int32).at[flat_e].add(1)
    padded = ((counts + MOE_BLOCK - 1) // MOE_BLOCK) * MOE_BLOCK
    pad_end = jnp.cumsum(padded)
    pad_start = pad_end - padded
    start = jnp.cumsum(counts) - counts
    rank = jnp.arange(a, dtype=jnp.int32) - start[sorted_e]
    dest = pad_start[sorted_e] + rank
    n_slots = a + N_EXPERTS * MOE_BLOCK
    n_blocks = n_slots // MOE_BLOCK
    slot_tok = jnp.zeros((n_slots,), jnp.int32).at[dest].set(flat_tok[order])
    slot_gate = jnp.zeros((n_slots,), jnp.float32).at[dest].set(flat_gate[order])
    block_e = jnp.clip(jnp.searchsorted(pad_end, jnp.arange(n_blocks, dtype=jnp.int32) * MOE_BLOCK, side='right'), 0, N_EXPERTS - 1)
    xs = xt[slot_tok].reshape(n_blocks, MOE_BLOCK, d)

    def expert_block(args):
        xb, e = args
        hgu = xb @ w_up_gate[e] + b_up_gate[e]
        x_glu = jnp.minimum(hgu[:, :D_EXPERT], SWIGLU_LIMIT)
        x_lin = jnp.clip(hgu[:, D_EXPERT:], -SWIGLU_LIMIT, SWIGLU_LIMIT)
        hact = x_glu * jax.nn.sigmoid(SWIGLU_ALPHA * x_glu) * (x_lin + 1.0)
        return hact @ w_down[e] + b_down[e]

    ys = lax.map(expert_block, (xs, block_e)).reshape(n_slots, d)
    return jnp.zeros((t, d), xt.dtype).at[slot_tok].add(ys * slot_gate[:, None].astype(xt.dtype))

def first_inputs(seed: int = 0) -> dict:
    key = jax.random.key(seed)
    ks = jax.random.split(key, 24)
    nrm = lambda k, shape, s: jax.random.normal(k, shape, jnp.float32) * s
    L = DEPTH
    return {
        "x": nrm(ks[0], (BATCH, SEQ, D_MODEL), 1.0),
        "p": nrm(ks[1], (DEPTH, BATCH, SEQ, PLE_DIM), 1.0),
        "positions": jnp.broadcast_to(jnp.arange(SEQ, dtype=jnp.int32), (BATCH, SEQ)),
        "g_mix_norm": 1.0 + nrm(ks[2], (L, D_MODEL), 0.02),
        "w_in": nrm(ks[3], (L, D_MODEL, D_IN), D_MODEL ** -0.5),
        "sb_q_gain": 1.0 + nrm(ks[4], (L, HEAD_DIM), 0.02),
        "sb_k_gain": 1.0 + nrm(ks[5], (L, HEAD_DIM), 0.02),
        "ret_q_gain": 1.0 + nrm(ks[6], (L, HEAD_DIM), 0.02),
        "ret_k_gain": 1.0 + nrm(ks[7], (L, HEAD_DIM), 0.02),
        "ret_gn_gain": 1.0 + nrm(ks[8], (L, RET_WIDTH), 0.02),
        "ret_gn_bias": nrm(ks[9], (L, RET_WIDTH), 0.02),
        "w_out": nrm(ks[10], (L, D_MIX, D_MODEL), D_MIX ** -0.5),
        "g_ffn_norm": 1.0 + nrm(ks[11], (L, D_MODEL), 0.02),
        "w_router": nrm(ks[12], (L, D_MODEL, N_EXPERTS), D_MODEL ** -0.5),
        "b_router": nrm(ks[13], (L, N_EXPERTS), 0.01),
        "w_up_gate": nrm(ks[14], (L, N_EXPERTS, D_MODEL, 2 * D_EXPERT), D_MODEL ** -0.5),
        "b_up_gate": nrm(ks[15], (L, N_EXPERTS, 2 * D_EXPERT), 0.02),
        "w_down": nrm(ks[16], (L, N_EXPERTS, D_EXPERT, D_MODEL), D_EXPERT ** -0.5),
        "b_down": nrm(ks[17], (L, N_EXPERTS, D_MODEL), 0.02),
        "g_ple_norm": 1.0 + nrm(ks[18], (L, D_MODEL), 0.02),
        "w_ple_gate": nrm(ks[19], (L, D_MODEL, D_MODEL), D_MODEL ** -0.5),
        "w_ple_proj": nrm(ks[20], (L, PLE_DIM, D_MODEL), PLE_DIM ** -0.5),
    }

def first_block(x, p, positions, g_mix_norm, w_in, sb_q_gain, sb_k_gain, ret_q_gain, ret_k_gain,
              ret_gn_gain, ret_gn_bias, w_out, g_ffn_norm, w_router, b_router, w_up_gate, b_up_gate,
              w_down, b_down, g_ple_norm, w_ple_gate, w_ple_proj):
    b, s, d = x.shape
    for i in range(DEPTH):
        xn = _rmsnorm(x, g_mix_norm[i])
        proj = xn @ w_in[i]
        o = 0
        sb_q = proj[..., o:o + SB_WIDTH]; o += SB_WIDTH
        sb_k = proj[..., o:o + SB_WIDTH]; o += SB_WIDTH
        sb_v = proj[..., o:o + SB_WIDTH]; o += SB_WIDTH
        r_q = proj[..., o:o + RET_WIDTH]; o += RET_WIDTH
        r_k = proj[..., o:o + RET_WIDTH]; o += RET_WIDTH
        r_v = proj[..., o:o + RET_WIDTH]; o += RET_WIDTH
        r_g = proj[..., o:o + RET_WIDTH]
        q_a = _rmsnorm(_heads(sb_q, SB_HEADS), sb_q_gain[i])
        k_a = _rmsnorm(_heads(sb_k, SB_HEADS), sb_k_gain[i])
        y_a = _stick_breaking(q_a, k_a, _heads(sb_v, SB_HEADS))
        y_a = y_a.transpose(0, 2, 1, 3).reshape(b, s, SB_WIDTH)
        q_b = _rope(_rmsnorm(_heads(r_q, RET_HEADS), ret_q_gain[i]), positions)
        k_b = _rope(_rmsnorm(_heads(r_k, RET_HEADS), ret_k_gain[i]), positions) * (HEAD_DIM ** -0.5)
        y_b = _retention(q_b, k_b, _heads(r_v, RET_HEADS))
        y_b = _group_norm(y_b, ret_gn_gain[i], ret_gn_bias[i]) * jax.nn.silu(r_g)
        x = x + jnp.concatenate([y_a, y_b], axis=-1) @ w_out[i]
        hn = _rmsnorm(x, g_ffn_norm[i]).reshape(b * s, d)
        x = x + _moe(hn, w_router[i], b_router[i], w_up_gate[i], b_up_gate[i], w_down[i], b_down[i]).reshape(b, s, d)
        gate = jax.nn.sigmoid(_rmsnorm(x, g_ple_norm[i]) @ w_ple_gate[i])
        x = x + (p[i] @ w_ple_proj[i]) * gate
    return x


GRID_W = 64
N_Q_HEADS = 8
N_KV_HEADS = 2
Q_PER_KV = N_Q_HEADS // N_KV_HEADS
ATTN_WIDTH = N_Q_HEADS * HEAD_DIM
KV_WIDTH = N_KV_HEADS * HEAD_DIM
ROPE_THETA = 10000.0
AXIAL_DIM = HEAD_DIM // 2
SSD_D_INNER = D_MODEL
SSD_HEADDIM = 64
SSD_HEADS = SSD_D_INNER // SSD_HEADDIM
SSD_GROUPS = 2
SSD_HEADS_PER_GROUP = SSD_HEADS // SSD_GROUPS
SSD_STATE = 128
CONV_K = 5
CHUNK = 128
CONV_CH = SSD_D_INNER + 2 * SSD_GROUPS * SSD_STATE
N_BRANCH = 2
D_FF = ((8 * D_MODEL // 3 + 255) // 256) * 256
IN_SPLITS = (ATTN_WIDTH, KV_WIDTH, KV_WIDTH, SSD_D_INNER, CONV_CH, 2 * SSD_HEADS, N_BRANCH * D_MODEL)
D_IN_PROJ = sum(IN_SPLITS)


def rms_norm(x, g):
    xf = x.astype(jnp.float32)
    xf = xf * lax.rsqrt(jnp.mean(xf * xf, axis=-1, keepdims=True) + EPS)
    return (xf * g.astype(jnp.float32)).astype(x.dtype)

def split_cols(h, sizes):
    idx = np.cumsum(np.array(sizes[:-1]))
    return jnp.split(h, [int(i) for i in idx], axis=-1)

def axial_angles(seq_len):
    rows = seq_len // GRID_W
    row_idx = jnp.repeat(jnp.arange(rows, dtype=jnp.float32), GRID_W)
    col_idx = jnp.tile(jnp.arange(GRID_W, dtype=jnp.float32), rows)
    inv_freq = ROPE_THETA ** (-jnp.arange(0, AXIAL_DIM, 2, dtype=jnp.float32) / AXIAL_DIM)
    ang_row = row_idx[:, None] * inv_freq[None, :]
    ang_col = col_idx[:, None] * inv_freq[None, :]
    return ang_row, ang_col

def rotate(xh, ang):
    half = xh.shape[-1] // 2
    x1, x2 = xh[..., :half], xh[..., half:]
    cos, sin = jnp.cos(ang).astype(xh.dtype), jnp.sin(ang).astype(xh.dtype)
    return jnp.concatenate([x1 * cos - x2 * sin, x2 * cos + x1 * sin], axis=-1)

def axial_rope(x, ang_row, ang_col):
    shp = (1, x.shape[1]) + (1,) * (x.ndim - 3) + (AXIAL_DIM // 2,)
    xr = rotate(x[..., :AXIAL_DIM], ang_row.reshape(shp))
    xc = rotate(x[..., AXIAL_DIM:], ang_col.reshape(shp))
    return jnp.concatenate([xr, xc], axis=-1)

def gqa_attention(q, k, v):
    b, s = q.shape[0], q.shape[1]
    nblk = s // Q_BLOCK
    scale = 1.0 / math.sqrt(HEAD_DIM)
    qb = jnp.moveaxis(q.reshape(b, nblk, Q_BLOCK, N_KV_HEADS, Q_PER_KV, HEAD_DIM), 1, 0)

    def block(q_blk):
        sc = jnp.einsum("bqkgd,bskd->bkgqs", q_blk, k).astype(jnp.float32) * scale
        p = jax.nn.softmax(sc, axis=-1).astype(v.dtype)
        return jnp.einsum("bkgqs,bskd->bqkgd", p, v)

    out = lax.map(block, qb)
    return jnp.moveaxis(out, 0, 1).reshape(b, s, ATTN_WIDTH)

def ssd_chunked(xs, dt, a, bm, cm):
    b, l, g, r, p = xs.shape
    n = bm.shape[-1]
    c = l // CHUNK
    xd = (xs * dt[..., None]).reshape(b, c, CHUNK, g, r, p)
    adt = jnp.moveaxis((dt * a).reshape(b, c, CHUNK, g, r), 2, -1)
    bc = bm.reshape(b, c, CHUNK, g, n)
    cc = cm.reshape(b, c, CHUNK, g, n)
    a_cs = jnp.cumsum(adt, axis=-1)
    tri = jnp.tril(jnp.ones((CHUNK, CHUNK), dtype=bool))
    seg = a_cs[..., :, None] - a_cs[..., None, :]
    decay_in = jnp.exp(jnp.where(tri, seg, -jnp.inf))
    cb = jnp.einsum("bclgn,bcsgn->bcgls", cc, bc)
    y_diag = jnp.einsum("bcgls,bcgrls,bcsgrp->bclgrp", cb, decay_in, xd)
    decay_states = jnp.exp(a_cs[..., -1:] - a_cs)
    states = jnp.einsum("bclgn,bcgrl,bclgrp->bcgrpn", bc, decay_states, xd)
    chunk_decay = jnp.exp(a_cs[..., -1])

    def step(h, inp):
        st, dec = inp
        return h * dec[..., None, None] + st, h

    h0 = jnp.zeros((b, g, r, p, n), dtype=xs.dtype)
    _, prev = lax.scan(step, h0, (jnp.moveaxis(states, 1, 0), jnp.moveaxis(chunk_decay, 1, 0)))
    prev = jnp.moveaxis(prev, 0, 1)
    y_off = jnp.einsum("bclgn,bcgrpn,bcgrl->bclgrp", cc, prev, jnp.exp(a_cs))
    return (y_diag + y_off).reshape(b, l, g, r, p)

def centred_depthwise_conv(u, w, bias):
    pad = (CONV_K - 1) // 2
    out = lax.conv_general_dilated(
        u, w[:, None, :].astype(u.dtype), window_strides=(1,), padding=[(pad, pad)],
        dimension_numbers=("NWC", "WIO", "NWC"), feature_group_count=u.shape[-1])
    return out + bias

def ssd_branch(z, xbc, dt_raw, conv_w, conv_b, dt_bias_f, dt_bias_b, a_log_f, a_log_b, d_skip, ssd_norm):
    b, l, _ = z.shape
    xbc = jax.nn.silu(centred_depthwise_conv(xbc, conv_w, conv_b))
    xs, bm, cm = split_cols(xbc, (SSD_D_INNER, SSD_GROUPS * SSD_STATE, SSD_GROUPS * SSD_STATE))
    f32 = jnp.float32
    xs = xs.astype(f32).reshape(b, l, SSD_GROUPS, SSD_HEADS_PER_GROUP, SSD_HEADDIM)
    bm = bm.astype(f32).reshape(b, l, SSD_GROUPS, SSD_STATE)
    cm = cm.astype(f32).reshape(b, l, SSD_GROUPS, SSD_STATE)
    dt_raw = dt_raw.astype(f32)
    shp = (SSD_GROUPS, SSD_HEADS_PER_GROUP)
    dt_f = jax.nn.softplus(dt_raw[..., :SSD_HEADS] + dt_bias_f.astype(f32)).reshape(b, l, *shp)
    dt_b = jax.nn.softplus(dt_raw[..., SSD_HEADS:] + dt_bias_b.astype(f32)).reshape(b, l, *shp)
    a_f = -jnp.exp(a_log_f.astype(f32)).reshape(shp)
    a_b = -jnp.exp(a_log_b.astype(f32)).reshape(shp)
    y_fwd = ssd_chunked(xs, dt_f, a_f, bm, cm)
    flip = lambda t: jnp.flip(t, axis=1)
    y_bwd = flip(ssd_chunked(flip(xs), flip(dt_b), a_b, flip(bm), flip(cm)))
    y = y_fwd + y_bwd + d_skip.astype(f32).reshape(shp)[..., None] * xs
    y = y.reshape(b, l, SSD_D_INNER).astype(z.dtype)
    return rms_norm(y * jax.nn.silu(z), ssd_norm)

def second_inputs(seed: int = 0) -> dict:
    key = jax.random.key(seed)
    ks = jax.random.split(key, 24)
    L = DEPTH
    nrm = lambda k, shape, fan_in: jax.random.normal(k, shape, jnp.float32) * fan_in ** -0.5
    gain = lambda k, shape: 1.0 + 0.05 * jax.random.normal(k, shape, jnp.float32)
    dt0 = jnp.exp(jax.random.uniform(ks[6], (2, L, SSD_HEADS), jnp.float32, math.log(1e-3), math.log(1e-1)))
    dt_bias = dt0 + jnp.log(-jnp.expm1(-dt0))
    a_log = jnp.log(jax.random.uniform(ks[7], (2, L, SSD_HEADS), jnp.float32, 1.0, 16.0))
    return {
        "x": jax.random.normal(ks[0], (BATCH, SEQ, D_MODEL), jnp.float32),
        "w_in": nrm(ks[1], (L, D_MODEL, D_IN_PROJ), D_MODEL),
        "q_norm": gain(ks[2], (L, HEAD_DIM)),
        "k_norm": gain(ks[3], (L, HEAD_DIM)),
        "conv_w": nrm(ks[4], (L, CONV_K, CONV_CH), CONV_K),
        "conv_b": 0.02 * jax.random.normal(ks[5], (L, CONV_CH), jnp.float32),
        "dt_bias_f": dt_bias[0],
        "dt_bias_b": dt_bias[1],
        "a_log_f": a_log[0],
        "a_log_b": a_log[1],
        "d_skip": 1.0 + 0.1 * jax.random.normal(ks[8], (L, SSD_HEADS), jnp.float32),
        "ssd_norm": gain(ks[9], (L, SSD_D_INNER)),
        "w_attn_proj": nrm(ks[10], (L, ATTN_WIDTH, D_MODEL), ATTN_WIDTH),
        "w_ssd_proj": nrm(ks[11], (L, SSD_D_INNER, D_MODEL), SSD_D_INNER),
        "w_out": nrm(ks[12], (L, D_MODEL, D_MODEL), D_MODEL),
        "norm1_pre": gain(ks[13], (L, D_MODEL)),
        "norm1_post": gain(ks[14], (L, D_MODEL)),
        "norm2_pre": gain(ks[15], (L, D_MODEL)),
        "norm2_post": gain(ks[16], (L, D_MODEL)),
        "w_gate_up": nrm(ks[17], (L, D_MODEL, 2 * D_FF), D_MODEL),
        "w_down": nrm(ks[18], (L, D_FF, D_MODEL), D_FF),
    }

def second_block(x, w_in, q_norm, k_norm, conv_w, conv_b, dt_bias_f, dt_bias_b, a_log_f, a_log_b,
              d_skip, ssd_norm, w_attn_proj, w_ssd_proj, w_out, norm1_pre, norm1_post,
              norm2_pre, norm2_post, w_gate_up, w_down):
    b, s, _ = x.shape
    ang_row, ang_col = axial_angles(s)
    for i in range(DEPTH):
        h = rms_norm(x, norm1_pre[i])
        proj = h @ w_in[i]
        q, k, v, z, xbc, dt_raw, gates = split_cols(proj, IN_SPLITS)
        q = rms_norm(q.reshape(b, s, N_KV_HEADS, Q_PER_KV, HEAD_DIM), q_norm[i])
        k = rms_norm(k.reshape(b, s, N_KV_HEADS, HEAD_DIM), k_norm[i])
        v = v.reshape(b, s, N_KV_HEADS, HEAD_DIM)
        q = axial_rope(q, ang_row, ang_col)
        k = axial_rope(k, ang_row, ang_col)
        attn_out = gqa_attention(q, k, v) @ w_attn_proj[i]
        ssd_y = ssd_branch(z, xbc, dt_raw, conv_w[i], conv_b[i], dt_bias_f[i], dt_bias_b[i],
                           a_log_f[i], a_log_b[i], d_skip[i], ssd_norm[i])
        ssd_out = ssd_y @ w_ssd_proj[i]
        g_attn, g_ssd = jnp.split(jax.nn.sigmoid(gates), N_BRANCH, axis=-1)
        mixed = (g_attn * attn_out + g_ssd * ssd_out) @ w_out[i]
        x = x + rms_norm(mixed, norm1_post[i])
        h2 = rms_norm(x, norm2_pre[i])
        gate, up = jnp.split(h2 @ w_gate_up[i], 2, axis=-1)
        ffn = (jax.nn.silu(gate) * up) @ w_down[i]
        x = x + rms_norm(ffn, norm2_post[i])
    return x


def setup_inputs(seed=0):
    out = dict(first_inputs(seed))
    for name, value in second_inputs(seed + 1).items():
        if name != "x":
            out[name + "_2"] = value
    return out


def reference(
    x, p, positions, g_mix_norm, w_in, sb_q_gain, sb_k_gain, ret_q_gain, ret_k_gain,
    ret_gn_gain, ret_gn_bias, w_out, g_ffn_norm, w_router, b_router, w_up_gate, b_up_gate,
    w_down, b_down, g_ple_norm, w_ple_gate, w_ple_proj, w_in_2, q_norm_2, k_norm_2, conv_w_2,
    conv_b_2, dt_bias_f_2, dt_bias_b_2, a_log_f_2, a_log_b_2, d_skip_2, ssd_norm_2,
    w_attn_proj_2, w_ssd_proj_2, w_out_2, norm1_pre_2, norm1_post_2, norm2_pre_2, norm2_post_2,
    w_gate_up_2, w_down_2,
):
    x = first_block(
        x, p, positions, g_mix_norm, w_in, sb_q_gain, sb_k_gain, ret_q_gain, ret_k_gain,
        ret_gn_gain, ret_gn_bias, w_out, g_ffn_norm, w_router, b_router, w_up_gate, b_up_gate,
        w_down, b_down, g_ple_norm, w_ple_gate, w_ple_proj,
    )
    return second_block(
        x, w_in_2, q_norm_2, k_norm_2, conv_w_2, conv_b_2, dt_bias_f_2, dt_bias_b_2, a_log_f_2,
        a_log_b_2, d_skip_2, ssd_norm_2, w_attn_proj_2, w_ssd_proj_2, w_out_2, norm1_pre_2,
        norm1_post_2, norm2_pre_2, norm2_post_2, w_gate_up_2, w_down_2,
    )


_drawn_inputs = setup_inputs


def setup_inputs(seed=0):
    import zlib

    import numpy as np

    out = dict(_drawn_inputs(seed))
    spreads = {}
    factors = {'sb_q_gain': 2.984,
     'b_up_gate': 4.549,
     'b_down': 5.169,
     'g_ple_norm': 8.0,
     'q_norm_2': 8.0,
     'k_norm_2': 8.0,
     'conv_b_2': 2.752}
    for name, (base, spread) in spreads.items():
        noise = np.random.default_rng([zlib.crc32(name.encode()), seed]).standard_normal(out[name].shape)
        drawn = base * np.exp(spread * noise) if base else spread * noise
        out[name] = __import__('jax').numpy.asarray(drawn.astype(out[name].dtype))
    for name, factor in factors.items():
        out[name] = (out[name] * factor).astype(out[name].dtype)
    return out
```

```python
from contextlib import ExitStack

import numpy as np

import concourse.bass as bass
from concourse import mybir

F32 = mybir.dt.float32
I32 = mybir.dt.int32
U32 = mybir.dt.uint32
ALU = mybir.AluOpType
ACT = mybir.ActivationFunctionType
AX = mybir.AxisListType

P = 128
T = 256
NTB = T // P
D = 1024
KC = D // P
HD = 64
NH = 8
NSEG = 7
E = 32
TOPK = 4
CAP = 64
PASSES = T // CAP
DFF = 2816
FC = DFF // P
EPS = 1e-6
SLOT = 2048
RING = 12
PER_EXPERT = 12
CONVK = 5
CC = 12
SSDH = 16

C_ID, C_LE, C_GE, C_LT, C_GT, C_ONE = (i * P for i in range(6))
C_SBM = 6 * P
C_DM = C_SBM + 3 * P
C_SLOT = C_DM + NH * 2 * P
C_EXP = C_SLOT + PASSES * P
C_FRQ = C_EXP + E
C_COS = C_FRQ + HD // 2
C_SIN = C_COS + 2 * 32
C_EPS = C_SIN + 2 * 32
NCONST = C_EPS + 2

V_MIX, V_FFN, V_PLE, V_SSD, V_N1, V_N2 = (i * KC for i in range(6))
V_CW = 6 * KC
V_CB = V_CW + CONVK * CC
NVEC = V_CB + CC

B_SBQ, B_SBK, B_RQ, B_RK, B_Q2, B_K2 = (i * HD for i in range(6))
B_GG = 6 * HD
B_GB = B_GG + 512
B_RT = B_GB + 512
B_DTB = B_RT + E
B_ALOG = B_DTB + 2 * SSDH
B_DSK = B_ALOG + 2 * SSDH
NBC = B_DSK + SSDH

TWO_PI_INV = float(1.0 / (2 * np.pi))
PI2_A = 6.28125
PI2_B = float(np.float32(2 * np.pi - PI2_A))
PI2_C = float(2 * np.pi - PI2_A - np.float64(np.float32(2 * np.pi - PI2_A)))
ROUND = 12582912.0
PI_IN = 3.1415925


def constants():
    c = np.zeros((P, NCONST), np.float32)
    i = np.arange(P)
    row, col = i[:, None], i[None, :]
    c[:, C_ID:C_ID + P] = row == col
    c[:, C_LE:C_LE + P] = row <= col
    c[:, C_GE:C_GE + P] = row >= col
    c[:, C_LT:C_LT + P] = row < col
    c[:, C_GT:C_GT + P] = row > col
    c[:, C_ONE:C_ONE + P] = 1.0
    c[:, C_SBM:C_SBM + P] = -(row < col).astype(np.float32)
    c[:, C_SBM + P:C_SBM + 2 * P] = -1.0
    c[:, C_SBM + 2 * P:C_SBM + 3 * P] = -(row < col).astype(np.float32)
    log_g = np.log(1.0 - 2.0 ** (-5.0 - np.arange(NH)))
    for h in range(NH):
        at = C_DM + h * 2 * P
        diff = (col - row).astype(np.float64)
        c[:, at:at + P] = np.where(diff >= 0, np.exp(log_g[h] * np.maximum(diff, 0)), 0) * HD ** -0.5
        c[:, at + P:at + 2 * P] = np.exp(log_g[h] * (diff + P)) * HD ** -0.5
    for p in range(PASSES):
        c[:, C_SLOT + p * P:C_SLOT + (p + 1) * P] = CAP * p + col % CAP
    c[:, C_EXP:C_EXP + E] = np.arange(E)
    half = HD // 2
    c[:, C_FRQ:C_FRQ + half] = np.float32(10000.0) ** (-np.arange(half, dtype=np.float32) / half)
    inv = np.float32(10000.0) ** (-np.arange(0, half, 2, dtype=np.float32) / np.float32(half))
    for tb in range(NTB):
        t = tb * P + i
        ang = np.concatenate([(t // 64)[:, None].astype(np.float32) * inv, (t % 64)[:, None].astype(np.float32) * inv], 1)
        c[:, C_COS + tb * 32:C_COS + (tb + 1) * 32] = np.cos(ang)
        c[:, C_SIN + tb * 32:C_SIN + (tb + 1) * 32] = np.sin(ang)
    c[:, C_EPS] = EPS
    return c


def build_program(nc, a, out, n_experts=E, debug=None):
    w_in, w_out, w_up, w_down_e = a["w_in"][0], a["w_out"][0], a["w_up_gate"][0], a["w_down"][0]
    w_in2 = a["w_in_2"][0]

    pieces, number = [], {}

    def piece(name, src, chunks, width):
        number[name] = len(pieces)
        pieces.append((src.rearrange("(k p) n -> p k n", p=P), chunks, width))

    def column_groups(tag, w, col0, groups):
        for g in range(groups):
            for half in range(2):
                piece((tag, g, half), w[half * 512:(half + 1) * 512, col0 + g * 512:col0 + (g + 1) * 512], 4, 512)

    column_groups("in", w_in, 0, NSEG)
    column_groups("out", w_out, 0, 2)
    piece("router", a["w_router"][0], KC, E)
    before_experts = len(pieces)
    ROUNDS = E + (PASSES - 1) * E
    number_of = {}
    base_c = before_experts + PER_EXPERT * ROUNDS
    late = len(pieces)
    column_groups("ple_gate", a["w_ple_gate"][0], 0, 2)
    piece("ple_proj", a["w_ple_proj"][0], 2, D)
    for c in range(6):
        piece(("xbc", c), w_in2[:, 1792 + 256 * c:2048 + 256 * c], KC, 256)
    piece("dt", w_in2[:, 3328:3360], KC, 32)
    piece("kv", w_in2[:, 512:768], KC, 256)
    column_groups("q", w_in2, 0, 1)
    column_groups("gates", w_in2, 3360, 4)
    column_groups("z", w_in2, 768, 2)
    column_groups("ssd_proj", a["w_ssd_proj_2"][0], 0, 2)
    for g in range(2):
        piece(("attn_proj", g), a["w_attn_proj_2"][0][:, g * 512:(g + 1) * 512], 4, 512)
    column_groups("out2", a["w_out_2"][0], 0, 2)
    w_gu = a["w_gate_up_2"][0]
    for j in range(FC // 2):
        piece(("gate", j), w_gu[:, 256 * j:256 * (j + 1)], KC, 256)
        piece(("up", j), w_gu[:, DFF + 256 * j:DFF + 256 * (j + 1)], KC, 256)
    for j in range(FC // 2):
        piece(("ffn_down", j), a["w_down_2"][0][256 * j:256 * (j + 1), :], 2, D)
    place = {k: n if n < late else n - late + base_c for k, n in number.items()}

    with ExitStack() as ctx:
        def sb(name, cols, dt=F32, parts=P):
            return ctx.enter_context(nc.sbuf_tensor(name, [parts, cols], dt))

        sems = {}

        def sem(name):
            return sems[name]

        names = ("consts vecs gains x_in late_in post2_in w_used dve_step act_step vecT_ps vecT "
                 "rms_sum rms xn xnT_ps xnT_dve xnT_act proj_sb head_sq head_sd "
                 "qkT_ps qkT sb_z sb_a sb_l sb_m sb_tail sb_t sb_e sb_w sb_pv yt trig_r trig "
                 "ret_qk ret_s ret_w ret_y silu_g yb ybT_ps ybT x1 "
                 "neg_max ex mask pos_ps flags gates gT_ps gT acc0 "
                 "onehot weighted sel gathered spread x_slots glu sig h_done hT_ps hT sT_slots y_slots scattered "
                 "ov_onehot ov_gathered ov_x ov_glu ov_sig ov_h ov_hT_ps ov_hT ov_y pass_end "
                 "x2 pT_ps pT ple_gate x3 xbc_sb dt_abs dt_sp a_exp adt cum_ps cum_done kv_sb q_sb conv silu_c "
                 "qk2 qk2T_ps qk2T s_ps s_max p_exp pT2_ps pT2 o_ps att attT_ps attT gate2 "
                 "xs_ps xs cb_ps cb z_sb abc e_sub e_exp w_ssd y_ssd y_mul ssd_xn mixed mixT_ps mixT_dve mixT_act "
                 "post_sd x4 silu_f ffn_act out_stored done").split()
        for n in names:
            sems[n] = ctx.enter_context(nc.semaphore(n))
        landed = [ctx.enter_context(nc.semaphore(f"landed{s}")) for s in range(RING)]

        ring = sb("ring", RING * SLOT)
        cst = sb("cst", NCONST)
        bc = sb("bc", NBC)
        arena = sb("arena", 22 * 1024)
        vecT = sb("vecT", NVEC)
        rope = sb("rope", 128)
        stat = sb("stat", 128)
        slot_of = sb("slot_of", 2 * (E + 1))
        gate_of = sb("gate_of", 2 * (E + 1))
        flag_i = sb("flag_i", 100, I32, 1)
        pos_i = sb("pos_i", 2, I32)
        top_i = sb("top_i", 16, U32)
        top_v = sb("top_v", 16)
        PS = ctx.enter_context(nc.psum_tensor("PS", [P, 8, 512], F32))

        def cc(at, n=P, parts=P):
            return cst[0:parts, at:at + n]

        ident = cc(C_ID)

        def area(at, n, parts=P):
            return arena[0:parts, at:at + n]

        def t3(ap, b):
            return ap.rearrange("p (b n) -> p b n", b=b)

        def banks(b, n):
            return PS[:, b:b + n, :].rearrange("p b n -> p (b n)")

        X = area(0, 2048)
        XN = area(2048, 2048)
        XNT = area(4096, 2048)
        PR = [area(6144 + 1024 * g, 1024) for g in range(NSEG)]
        QKT = [area(13312 + 1024 * s, 1024) for s in range(4)]
        YT = area(17408, 2048)
        SBT = [area(19456 + 768 * j, 768) for j in range(4)]
        WR = area(19456, 3072)
        YB = QKT[0]
        VECS = area(19456, P, NVEC)
        TMP = area(2048, 1024)
        ROT = [area(3072 + 256 * j, 256) for j in range(4)]
        BUP = area(6144, 2048, E)
        BDN = area(8192, 1024, E)
        XG = area(9216, 512)
        SPT = area(9728, 256)
        GLU, SIG, LIN, HH = (area(9984 + 512 * j, 512) for j in range(4))
        HTS = area(12032, 512)
        YS = area(12544, 512)
        OH = area(13056, 256)
        OHG = area(13312, 256)
        SEL = area(13568, 64, E)
        GTT = area(13696, 256, E)
        EXM = area(13952, 64)
        MASK = area(14016, 64)
        logit = area(14080, 64)
        flag_f = area(14144, 100, 1)
        PIN = area(14336, 512)
        PT = area(14848, 512)
        SG = area(6144, 2048)
        UB = area(6144, CC * 260).rearrange("p (c n) -> p c n", c=CC)
        XBT = area(9264, CC * 256).rearrange("p (c n) -> p c n", c=CC)
        QK = area(12336, 1280)
        VV = area(13616, 256)
        KD = area(13872, 512)
        ROT2 = [area(14384 + 320 * j, 320) for j in range(4)]
        QT = area(15664, 1024)
        KT = area(16688, 512)
        PE_ = area(6144, 1024)
        PTS = area(7168, 1024)
        ATT = area(8192, 1024)
        ATTT = area(14384, 1024)
        GATES = area(17200, 4096)
        N1P = area(21296, 1024)
        SQ2 = area(2048, 1280)
        Z = area(12336, 2048)
        CBM = area(15664, 1536)
        XS = area(9264, 2048)
        EE = [area(6144 + 768 * j, 768) for j in range(2)]
        WW = [area(7680 + 768 * j, 768) for j in range(2)]
        DT, ADT, CUM, CUMX, DTA = (area(2048 + 64 * j, 64) for j in range(20, 25))
        AEX = area(2048 + 64 * 25, 32)
        M1 = area(12336, 2048)
        ACTT = area(6144, FC * 256).rearrange("p (f t) -> p f t", f=FC)
        SF = [area(12336 + 512 * j, 512) for j in range(2)]
        N2P = area(14384, 1024)

        def slot(n):
            return ring[:, (n % RING) * SLOT:(n % RING + 1) * SLOT]

        def view(key):
            _, chunks, width = pieces[number[key]]
            n = place[key]
            return slot(n)[:, 0:chunks * width].rearrange("p (k n) -> p k n", k=chunks)

        def expert_slot(j):
            return slot(before_experts + j)

        def chain(eng, name):
            n = [0]

            def link(ins):
                n[0] += 1
                ins.then_inc(sem(name), 1)
                eng.wait_ge(sem(name), n[0])
            return link, n

        def bcast(ap, mid):
            return ap.unsqueeze(1).to_broadcast([ap.shape[0], mid, ap.shape[1]])

        def spread_last(ap, n):
            return ap.unsqueeze(2).to_broadcast([ap.shape[0], ap.shape[1], n])

        block = ctx.enter_context(nc.Block())

        @block.sync
        def _(sp):
            def load(key):
                src, chunks, width = pieces[number[key]]
                n = place[key]
                if n >= RING:
                    sp.wait_ge(sem("w_used"), n - RING + 1)
                sp.dma_start(view(key), src).then_inc(landed[n % RING], 16)

            keys = sorted(place, key=place.get)
            for key in keys:
                if place[key] < before_experts:
                    load(key)

            def expert_loads(e, turn):
                for j in range(PER_EXPERT):
                    n = before_experts + j
                    sp.wait_ge(sem("w_used"), turn * PER_EXPERT + (n - RING + 1))
                    if j < KC:
                        src = w_up[e, j * P:(j + 1) * P, :]
                    else:
                        src = w_down_e[e, (j - KC) * 256:(j - KC + 1) * 256, :].rearrange("(k p) n -> p k n", p=P)
                    dst = expert_slot(j)
                    if j >= KC:
                        dst = dst.rearrange("p (k n) -> p k n", k=2)
                    sp.dma_start(dst, src).then_inc(landed[n % RING], 16)

            with sp.Fori(0, n_experts) as e:
                expert_loads(e, e)
            sp.wait_ge(sem("flags"), 1)
            any_more = sp.value_load(flag_i[0:1, 96:97])
            with sp.If(any_more > 0):
                with sp.Fori(0, PASSES - 1) as p:
                    with sp.Fori(0, E) as e:
                        more = sp.value_load(flag_i[0:1, bass.ds(p * E + e, 1)])
                        with sp.If(more > 0):
                            expert_loads(e, p * E + e + E)
                            sp.wait_ge(sem("w_used"), (p * E + e) * PER_EXPERT + (before_experts + PER_EXPERT * (E + 1)))
                            sp.sem_inc(sem("pass_end"), 1)
                        with sp.Else():
                            sp.wait_ge(sem("w_used"), (p * E + e) * PER_EXPERT + (before_experts + PER_EXPERT * E))
                            for j in range(PER_EXPERT):
                                sp.sem_inc(landed[j], 16)
                        sp.nop()
                sp.nop()
            with sp.Else():
                sp.wait_ge(sem("w_used"), before_experts + PER_EXPERT * n_experts)
                for j in range(PER_EXPERT):
                    sp.sem_inc(landed[j], 16 * (PASSES - 1) * E)
            sp.nop()
            for key in keys:
                if place[key] >= before_experts:
                    load(key)
            sp.wait_ge(sem("done"), 2)
            sp.dma_start(out[0].rearrange("(b p) d -> p b d", p=P), t3(X, 2)).then_inc(sem("out_stored"), 16)
            sp.wait_ge(sem("out_stored"), 16)

        @block.tensor
        def _(pe):
            def arrived(key):
                n = place[key]
                pe.wait_ge(landed[n % RING], 16 * (n // RING + 1))

            def transposes(src, bank, sem_name, per_signal=4):
                for c in range(KC):
                    for tb in range(NTB):
                        ins = nc.tensor.transpose(PS[:, bank + c // 2, (c % 2) * 256 + tb * P:(c % 2) * 256 + (tb + 1) * P],
                                                  t3(src, 2)[:, tb, c * P:(c + 1) * P], ident)
                    if c % 2:
                        ins.then_inc(sem(sem_name), 1)

            def half_transposes(src, bank, sem_name):
                for c in range(4):
                    for tb in range(NTB):
                        ins = nc.tensor.transpose(PS[:, bank + c // 2, (c % 2) * 256 + tb * P:(c % 2) * 256 + (tb + 1) * P],
                                                  t3(src, 2)[:, tb, c * P:(c + 1) * P], ident)
                ins.then_inc(sem(sem_name), 1)

            def norm_T(i):
                pe.wait_ge(sem("xn"), 2 * (i + 1))
                transposes(XN, 4, "xnT_ps")

            def need_xnT(i):
                pe.wait_ge(sem("xnT_dve"), 2 * (i + 1))
                pe.wait_ge(sem("xnT_act"), 2 * (i + 1))

            def half_group(tag, g, half, lhs, bank_of, chunks=4, first=0, last=7):
                key = (tag, g, half) if half is not None else (tag, g)
                arrived(key)
                w = view(key)
                h = half or 0
                for tb in range(NTB):
                    for k in range(4):
                        c = h * 4 + k
                        ins = nc.tensor.matmul(PS[:, bank_of(tb), :], lhs[:, c * 256 + tb * P:c * 256 + (tb + 1) * P],
                                               w[:, k, :], start=c == first, stop=c == last)
                ins.then_inc(sem("w_used"), 1)

            pe.wait_ge(sem("consts"), 16)
            pe.wait_ge(sem("vecs"), 128)
            nc.tensor.transpose(PS[:, 0, 0:NVEC], VECS, cst[0:NVEC, C_ID:C_ID + NVEC]).then_inc(sem("vecT_ps"), 1)
            norm_T(0)
            need_xnT(0)
            def seg(g, half):
                if half == 0 and g >= 2:
                    pe.wait_ge(sem("proj_sb"), g - 1)
                half_group("in", g, half, XNT, lambda tb: 2 * (g % 2) + tb)

            def sb_z(b):
                if b == 0:
                    pe.wait_ge(sem("qkT"), 2)
                else:
                    pe.wait_ge(sem("yt"), b)
                for hh in range(2):
                    q = t3(QKT[0], 4)[64 * hh:64 * hh + 64, b, :]
                    k = t3(QKT[1], 4)[64 * hh:64 * hh + 64, b, :]
                    nc.tensor.matmul(PS[:, 4 + hh, 0:256], k[:, 0:P], q, start=True, stop=True)
                    ins = nc.tensor.matmul(PS[:, 4 + hh, 256:384], k[:, P:256], q[:, P:256], start=True, stop=True)
                ins.then_inc(sem("sb_z"), 1)

            def sb_tail(b):
                pe.wait_ge(sem("sb_m"), b + 1)
                m = t3(SBT[2], 2)
                for hh in range(2):
                    nc.tensor.matmul(PS[:, 6 + hh, 0:256], cc(C_GT), m[:, hh, 0:256], start=True, stop=False)
                    nc.tensor.matmul(PS[:, 6 + hh, P:256], cc(C_ONE), m[:, hh, 256:384], start=False, stop=True)
                    ins = nc.tensor.matmul(PS[:, 6 + hh, 256:384], cc(C_GT), m[:, hh, 256:384], start=True, stop=True)
                ins.then_inc(sem("sb_tail"), 1)

            def sb_pv(b):
                pe.wait_ge(sem("sb_w"), b + 1)
                w, v = t3(SBT[3], 2), t3(PR[2], 2)
                for hh in range(2):
                    c0 = (2 * b + hh) * HD
                    nc.tensor.matmul(PS[64 * hh:64 * hh + 64, 4, 0:256], v[:, 0, c0:c0 + HD], w[:, hh, 0:256], start=True, stop=False)
                    ins = nc.tensor.matmul(PS[64 * hh:64 * hh + 64, 4, P:256], v[:, 1, c0:c0 + HD], w[:, hh, 256:384], start=False, stop=True)
                ins.then_inc(sem("sb_pv"), 1)

            seg(0, 0), seg(0, 1), seg(1, 0), seg(1, 1)
            pe.wait_ge(sem("ret_qk"), 1)
            half_transposes(PR[0], 4, "qkT_ps")
            seg(2, 0), seg(2, 1)
            pe.wait_ge(sem("ret_qk"), 2)
            half_transposes(PR[1], 6, "qkT_ps")
            for b in range(4):
                sb_z(b)
                seg(3 + b, 0)
                sb_tail(b)
                seg(3 + b, 1)
                sb_pv(b)
            pe.wait_ge(sem("ret_qk"), 3)
            half_transposes(PR[3], 6, "qkT_ps")
            pe.wait_ge(sem("ret_qk"), 4)
            pe.wait_ge(sem("yt"), 4)
            half_transposes(PR[4], 4, "qkT_ps")
            pe.wait_ge(sem("qkT"), 4)
            pe.wait_ge(sem("proj_sb"), NSEG)

            def ret_scores(h):
                if h >= 4:
                    pe.wait_ge(sem("ret_w"), h - 3)
                q = t3(QKT[2], 4)[64 * (h % 2):64 * (h % 2) + 64, h // 2, :]
                k = t3(QKT[3], 4)[64 * (h % 2):64 * (h % 2) + 64, h // 2, :]
                nc.tensor.matmul(PS[:, h % 4, 0:256], k[:, 0:P], q, start=True, stop=True)
                nc.tensor.matmul(PS[:, h % 4, 256:384], k[:, P:256], q[:, P:256], start=True, stop=True).then_inc(sem("ret_s"), 1)

            for h in range(4):
                ret_scores(h)
            v3 = t3(PR[5], 2)
            for h in range(NH):
                pe.wait_ge(sem("ret_w"), h + 1)
                w = WR[:, h * 384:(h + 1) * 384]
                c0, c1 = h * HD, (h + 1) * HD
                nc.tensor.matmul(PS[:, 4, c0:c1], w[:, 0:P], v3[:, 0, c0:c1], start=True, stop=True)
                nc.tensor.matmul(PS[:, 5, c0:c1], w[:, P:256], v3[:, 0, c0:c1], start=True, stop=False)
                ins = nc.tensor.matmul(PS[:, 5, c0:c1], w[:, 256:384], v3[:, 1, c0:c1], start=False, stop=True)
                if h + 4 < NH:
                    ret_scores(h + 4)
            ins.then_inc(sem("ret_y"), 1)
            pe.wait_ge(sem("yb"), 1)
            half_transposes(YB, 6, "ybT_ps")
            pe.wait_ge(sem("ybT"), 1)
            for g in range(2):
                for half in range(2):
                    half_group("out", g, half, YT, lambda tb: 2 * tb + g)
            norm_T(1)
            need_xnT(1)
            arrived("router")
            for tb in range(NTB):
                for k in range(KC):
                    ins = nc.tensor.matmul(PS[:, 0, tb * E:(tb + 1) * E], XNT[:, k * 256 + tb * P:k * 256 + (tb + 1) * P],
                                           view("router")[:, k, :], start=k == 0, stop=k == KC - 1)
            ins.then_inc(sem("w_used"), 1)
            pe.wait_ge(sem("mask"), 1)
            m = t3(MASK, 2)
            nc.tensor.matmul(PS[:, 1, 0:E], cc(C_LT), m[:, 0, :], start=True, stop=True)
            nc.tensor.matmul(PS[:, 1, E:2 * E], cc(C_ONE), m[:, 0, :], start=True, stop=False)
            nc.tensor.matmul(PS[:, 1, E:2 * E], cc(C_LT), m[:, 1, :], start=False, stop=True)
            nc.tensor.matmul(PS[:, 1, 2 * E:3 * E], cc(C_ONE), m[:, 0, :], start=True, stop=False)
            nc.tensor.matmul(PS[:, 1, 2 * E:3 * E], cc(C_ONE), m[:, 1, :], start=False, stop=True).then_inc(sem("pos_ps"), 1)
            pe.wait_ge(sem("gates"), 1)
            for tb in range(NTB):
                ins = nc.tensor.transpose(PS[0:E, 2, tb * P:(tb + 1) * P], t3(gate_of[:, :], 2)[:, tb, 0:E], ident)
            ins.then_inc(sem("gT_ps"), 1)
            pe.wait_ge(sem("gT"), 1)
            pe.wait_ge(sem("flags"), 1)
            pe.wait_ge(sem("late_in"), 48)
            for tb in range(NTB):
                for n in range(2):
                    nc.tensor.matmul(PS[:, 2 * tb + n, :], GTT[:, tb * P:(tb + 1) * P], BDN[:, n * 512:(n + 1) * 512],
                                     start=True, stop=False, skip_group_check=True)

            def gather(sig):
                for c in range(KC):
                    for tb in range(NTB):
                        ins = nc.tensor.matmul(PS[:, 6, c * CAP:(c + 1) * CAP], t3(XN, 2)[:, tb, c * P:(c + 1) * P],
                                               OH[:, tb * P:tb * P + CAP], start=tb == 0, stop=tb == 1)
                ins.then_inc(sem(sig), 1)

            def spread(sig):
                for tb in range(NTB):
                    ins = nc.tensor.transpose(PS[:, 7, tb * P:(tb + 1) * P], OHG[:, tb * P:(tb + 1) * P], ident)
                ins.then_inc(sem(sig), 1)

            def up(turn):
                for n in range(4):
                    nc.tensor.matmul(PS[64 * (n % 2):64 * (n % 2) + 64, 4 + n // 2, :], SEL, BUP[:, n * 512:(n + 1) * 512],
                                     start=True, stop=False)
                for c in range(KC):
                    n_ = before_experts + c
                    pe.wait_ge(landed[n_ % RING], turn * 16 + 16 * (n_ // RING + 1))
                    w = expert_slot(c)
                    for n in range(4):
                        ins = nc.tensor.matmul(PS[64 * (n % 2):64 * (n % 2) + 64, 4 + n // 2, :], XG[:, c * CAP:(c + 1) * CAP],
                                               w[:, n * 512:(n + 1) * 512], start=False, stop=c == KC - 1)
                    ins.then_inc(sem("w_used"), 1)

            def h_transposes(sig):
                for j in range(4):
                    ins = nc.tensor.transpose(PS[:, 6, j * P:(j + 1) * P], HH[:, j * P:(j + 1) * P], ident)
                ins.then_inc(sem(sig), 1)

            def down(turn):
                for j in range(4):
                    n_ = before_experts + KC + j
                    pe.wait_ge(landed[n_ % RING], turn * 16 + 16 * (n_ // RING + 1))
                    w = expert_slot(KC + j).rearrange("p (k n) -> p k n", k=2)
                    for k in range(2):
                        c = 2 * j + k
                        lhs = HTS[:, (c % 4) * P + CAP * (c // 4):(c % 4) * P + CAP * (c // 4) + CAP]
                        for n in range(2):
                            ins = nc.tensor.matmul(PS[64 * n:64 * n + 64, 7, :], lhs, w[:, k, n * 512:(n + 1) * 512],
                                                   start=c == 0, stop=c == KC - 1)
                    ins.then_inc(sem("w_used"), 1)

            def scatter(sig):
                for tb in range(NTB):
                    for n in range(2):
                        ins = nc.tensor.matmul(PS[:, 2 * tb + n, :], SPT[64 * n:64 * n + 64, tb * P:(tb + 1) * P],
                                               YS[64 * n:64 * n + 64, :], start=False, stop=False, skip_group_check=True)
                ins.then_inc(sem(sig), 1)

            pe.wait_ge(sem("onehot"), 1)
            gather("gathered")
            with pe.Fori(0, n_experts) as e:
                pe.wait_ge(sem("x_slots"), e + 1)
                pe.wait_ge(sem("sel"), e + 1)
                up(e)
                pe.wait_ge(sem("weighted"), e + 1)
                spread("spread")
                pe.wait_ge(sem("onehot"), e + 2)
                gather("gathered")
                pe.wait_ge(sem("h_done"), e + 1)
                pe.wait_ge(sem("x_slots"), e + 2)
                h_transposes("hT_ps")
                pe.wait_ge(sem("sT_slots"), e + 1)
                pe.wait_ge(sem("hT"), e + 1)
                down(e)
                pe.wait_ge(sem("y_slots"), e + 1)
                scatter("scattered")
            any_more = pe.value_load(flag_i[0:1, 96:97])
            with pe.If(any_more > 0):
                with pe.Fori(0, PASSES - 1) as p:
                    with pe.Fori(0, E) as e:
                        more = pe.value_load(flag_i[0:1, bass.ds(p * E + e, 1)])
                        with pe.If(more > 0):
                            t = p * E + e
                            pe.wait_ge(sem("ov_onehot"), t + 1)
                            gather("ov_gathered")
                            spread("ov_gathered")
                            pe.wait_ge(sem("ov_x"), t + 1)
                            up(t + E)
                            pe.wait_ge(sem("ov_h"), t + 1)
                            h_transposes("ov_hT_ps")
                            pe.wait_ge(sem("ov_hT"), t + 1)
                            down(t + E)
                            pe.wait_ge(sem("ov_y"), t + 1)
                            scatter("scattered")
                            pe.wait_ge(sem("scattered"), t + (n_experts + 1))
                            pe.sem_inc(sem("pass_end"), 1)
                        with pe.Else():
                            pe.sem_inc(sem("w_used"), PER_EXPERT)
                            pe.sem_inc(sem("ov_gathered"), 2)
                            pe.sem_inc(sem("ov_hT_ps"), 1)
                            pe.sem_inc(sem("scattered"), 1)
                        pe.nop()
                pe.nop()
            with pe.Else():
                pe.wait_ge(sem("scattered"), n_experts)
                pe.sem_inc(sem("w_used"), PER_EXPERT * (PASSES - 1) * E)
                pe.sem_inc(sem("scattered"), (PASSES - 1) * E)
            pe.nop()

            for kc in range(2):
                for tb in range(NTB):
                    ins = nc.tensor.transpose(PS[:, 6, kc * 256 + tb * P:kc * 256 + (tb + 1) * P],
                                              t3(PIN, 2)[:, tb, kc * P:(kc + 1) * P], ident)
            ins.then_inc(sem("pT_ps"), 1)
            pe.wait_ge(sem("pT"), 1)
            norm_T(2)
            need_xnT(2)
            for g in range(2):
                for half in range(2):
                    half_group("ple_gate", g, half, XNT, lambda tb: 2 * tb + g)
            arrived("ple_proj")
            w = view("ple_proj")
            for tb in range(NTB):
                for n in range(2):
                    for k in range(2):
                        ins = nc.tensor.matmul(PS[:, 4 + 2 * tb + n, :], PT[:, k * 256 + tb * P:k * 256 + (tb + 1) * P],
                                               w[:, k, n * 512:(n + 1) * 512], start=k == 0, stop=k == 1)
            ins.then_inc(sem("w_used"), 1)

            norm_T(3)
            need_xnT(3)

            def feature_rows(key, bank):
                arrived(key)
                w = view(key)
                for c in range(2):
                    for k in range(KC):
                        ins = nc.tensor.matmul(PS[:, bank, c * 256:(c + 1) * 256], w[:, k, c * P:(c + 1) * P],
                                               XNT[:, k * 256:(k + 1) * 256], start=k == 0, stop=k == KC - 1)
                ins.then_inc(sem("w_used"), 1)

            def token_rows(key, bank, width):
                arrived(key)
                w = view(key)
                for tb in range(NTB):
                    for k in range(KC):
                        ins = nc.tensor.matmul(PS[:, bank, tb * width:(tb + 1) * width],
                                               XNT[:, k * 256 + tb * P:k * 256 + (tb + 1) * P], w[:, k, :],
                                               start=k == 0, stop=k == KC - 1)
                ins.then_inc(sem("w_used"), 1)

            for c in range(6):
                feature_rows(("xbc", c), c)
            token_rows("dt", 6, 32)
            token_rows("kv", 7, 256)
            pe.wait_ge(sem("xbc_sb"), 2)
            for half in range(2):
                half_group("q", 0, half, XNT, lambda tb: tb)

            def gates(i):
                g, half = divmod(i, 2)
                if half == 0:
                    if g == 0:
                        pe.wait_ge(sem("kv_sb"), 1)
                        pe.wait_ge(sem("qk2T"), 1)
                    else:
                        pe.wait_ge(sem("gate2"), g)
                half_group("gates", g, half, XNT, lambda tb: 6 + tb)

            pe.wait_ge(sem("dt_sp"), 1)
            pe.wait_ge(sem("kv_sb"), 1)
            pe.wait_ge(sem("qk2"), 2)
            for c in range(4):
                for tb in range(NTB):
                    ins = nc.tensor.transpose(PS[:, 6 + c // 2, (c % 2) * 256 + tb * P:(c % 2) * 256 + (tb + 1) * P],
                                              t3(QK, 2)[:, tb, c * P:(c + 1) * P], ident)
            ins.then_inc(sem("qk2T_ps"), 1)
            pe.wait_ge(sem("xbc_sb"), 6)
            for kv in range(2):
                for tb in range(NTB):
                    ins = nc.tensor.transpose(PS[:, 2, kv * 256 + tb * P:kv * 256 + (tb + 1) * P],
                                              t3(KD, 2)[:, tb, kv * P:(kv + 1) * P], ident)
            ins.then_inc(sem("qk2T_ps"), 1)
            pe.wait_ge(sem("qk2T"), 2)
            pe.wait_ge(sem("q_sb"), 1)
            for u in range(4):
                tb, h0 = u // 2, 4 * (u % 2)
                if u >= 1:
                    pe.wait_ge(sem("p_exp"), 4 * u)
                for i in range(4):
                    h = h0 + i
                    r = 64 * (h % 2)
                    ins = nc.tensor.matmul(PS[:, i % 2, (i // 2) * 256:(i // 2) * 256 + 256],
                                           t3(QT, 4)[r:r + 64, h // 2, tb * P:(tb + 1) * P],
                                           t3(KT, 2)[r:r + 64, h // 4, :], start=True, stop=True)
                ins.then_inc(sem("s_ps"), 1)
                gates(2 * u)
                pe.wait_ge(sem("p_exp"), 4 * (u + 1))
                if u >= 1:
                    pe.wait_ge(sem("pT2"), u)
                for i in range(4):
                    for kb in range(2):
                        ins = nc.tensor.transpose(PS[:, 2 + i // 2, (i % 2) * 256 + kb * P:(i % 2) * 256 + (kb + 1) * P],
                                                  t3(PE_, 4)[:, i, kb * P:(kb + 1) * P], ident)
                ins.then_inc(sem("pT2_ps"), 1)
                gates(2 * u + 1)
                pe.wait_ge(sem("pT2"), u + 1)
                for i in range(4):
                    h = h0 + i
                    for kb in range(2):
                        ins = nc.tensor.matmul(PS[:, 4 + tb, h * HD:(h + 1) * HD], t3(PTS, 4)[:, i, kb * P:(kb + 1) * P],
                                               t3(VV, 2)[:, kb, (h // 4) * HD:(h // 4 + 1) * HD], start=kb == 0, stop=kb == 1)
                ins.then_inc(sem("o_ps"), 1)
            pe.wait_ge(sem("att"), 1)
            half_transposes(ATT, 4, "attT_ps")

            pe.wait_ge(sem("silu_c"), CC)
            for c in range(KC):
                for tb in range(NTB):
                    ins = nc.tensor.transpose(PS[:, 2 * tb + c // 4, (c % 4) * P:(c % 4 + 1) * P],
                                              XBT[:, c, tb * P:(tb + 1) * P], ident)
            ins.then_inc(sem("xs_ps"), 1)
            pe.wait_ge(sem("gate2"), 4)
            for g in range(2):
                for s in range(2):
                    ins = nc.tensor.matmul(PS[:, 6 + g, s * 256:(s + 1) * 256], XBT[:, 8 + g, s * P:(s + 1) * P],
                                           XBT[:, 10 + g, :], start=True, stop=True)
            ins.then_inc(sem("cb_ps"), 1)
            pe.wait_ge(sem("adt"), 1)
            pe.wait_ge(sem("attT"), 1)
            adt = t3(ADT, 2)
            for tb in range(NTB):
                nc.tensor.matmul(PS[:, 4, tb * 32:tb * 32 + 16], cc(C_LE), adt[:, tb, 0:16], start=True, stop=True)
                nc.tensor.matmul(PS[:, 4, tb * 32 + 16:tb * 32 + 32], cc(C_GE), adt[:, tb, 16:32], start=True, stop=True)
                ins = nc.tensor.matmul(PS[:, 4, 64 + tb * 32:96 + tb * 32], cc(C_ONE), adt[:, tb, :], start=True, stop=True)
            ins.then_inc(sem("cum_ps"), 1)
            pe.wait_ge(sem("cum_done"), 1)

            def abc(h):
                if h >= 2:
                    pe.wait_ge(sem("e_sub"), h - 1)
                for d in range(2):
                    for tb in range(NTB):
                        ins = nc.tensor.matmul(PS[:, 4 + h % 2, d * 256 + tb * P:d * 256 + (tb + 1) * P],
                                               adt[:, tb, d * 16 + h:d * 16 + h + 1].to_broadcast([P, P]),
                                               cc(C_LE if d == 0 else C_GE), start=True, stop=True)
                ins.then_inc(sem("abc"), 1)

            abc(0), abc(1)
            pe.wait_ge(sem("xs"), 1)
            pe.wait_ge(sem("cb"), 1)
            xs = t3(XS, 2)
            for h in range(SSDH):
                if h % 3 == 0 and h < 12:
                    g, half = divmod(h // 3, 2)
                    if half == 0 and g:
                        pe.wait_ge(sem("z_sb"), g)
                    half_group("z", g, half, XNT, lambda tb: 6 + tb)
                pe.wait_ge(sem("w_ssd"), h + 1)
                w = WW[h % 2]
                n, c0 = h // 8, (h % 8) * HD
                for tb, terms in ((0, ((0, 0), (3, 0), (5, 1))), (1, ((1, 0), (2, 1), (4, 1)))):
                    for i, (blk, s) in enumerate(terms):
                        ins = nc.tensor.matmul(PS[:, 2 * tb + n, c0:c0 + HD], w[:, blk * P:(blk + 1) * P],
                                               xs[:, s, h * HD:(h + 1) * HD], start=i == 0, stop=i == 2)
                ins.then_inc(sem("y_ssd"), 1)
                if h + 2 < SSDH:
                    abc(h + 2)
            norm_T(4)
            need_xnT(4)
            for g in range(2):
                for half in range(2):
                    half_group("ssd_proj", g, half, XNT, lambda tb: 2 * tb + g)
            for g in range(2):
                half_group("attn_proj", g, None, ATTT, lambda tb: 4 + 2 * tb + g, last=3)
            pe.wait_ge(sem("mixed"), 1)
            transposes(XN, 4, "mixT_ps")
            pe.wait_ge(sem("mixT_dve"), 2)
            pe.wait_ge(sem("mixT_act"), 2)
            for g in range(2):
                for half in range(2):
                    half_group("out2", g, half, XNT, lambda tb: 2 * tb + g)
            norm_T(5)
            need_xnT(5)
            for j in range(FC // 2):
                if j >= 4:
                    pe.wait_ge(sem("ffn_act"), j - 3)
                feature_rows(("gate", j), 2 * (j % 4))
                feature_rows(("up", j), 2 * (j % 4) + 1)
            pe.wait_ge(sem("ffn_act"), FC // 2 - 1)
            for j in range(FC // 2):
                if j == FC // 2 - 1:
                    pe.wait_ge(sem("ffn_act"), FC // 2)
                arrived(("ffn_down", j))
                w = view(("ffn_down", j))
                for k in range(2):
                    f = 2 * j + k
                    for tb in range(NTB):
                        for n in range(2):
                            ins = nc.tensor.matmul(PS[:, (2 * tb + n), :], ACTT[:, f, tb * P:(tb + 1) * P],
                                                   w[:, k, n * 512:(n + 1) * 512], start=f == 0, stop=f == FC - 1)
                ins.then_inc(sem("w_used"), 1)

        @block.scalar
        def _(act):
            link, _n = chain(act, "act_step")
            eps = cc(C_EPS, 1)

            act.dma_start(t3(X, 2), a["x"][0].rearrange("(b p) d -> p b d", p=P)).then_inc(sem("x_in"), 16)
            act.dma_start(cst[:, :], a["consts"]).then_inc(sem("consts"), 16)
            vec_rows = [(V_MIX, KC, a["g_mix_norm"][0].rearrange("(r n) -> r n", n=P)),
                        (V_FFN, KC, a["g_ffn_norm"][0].rearrange("(r n) -> r n", n=P)),
                        (V_PLE, KC, a["g_ple_norm"][0].rearrange("(r n) -> r n", n=P)),
                        (V_SSD, KC, a["ssd_norm_2"][0].rearrange("(r n) -> r n", n=P)),
                        (V_N1, KC, a["norm1_pre_2"][0].rearrange("(r n) -> r n", n=P)),
                        (V_N2, KC, a["norm2_pre_2"][0].rearrange("(r n) -> r n", n=P)),
                        (V_CW, CONVK * CC, a["conv_w_2"][0].rearrange("k (r n) -> (k r) n", n=P)),
                        (V_CB, CC, a["conv_b_2"][0].rearrange("(r n) -> r n", n=P))]
            for at, rows, src in vec_rows:
                act.dma_start(VECS[at:at + rows, :], src).then_inc(sem("vecs"), 16)
            act.dma_start(pos_i[:, :], a["positions"].rearrange("o (b p) -> p (o b)", p=P),
                          allow_slow_non_contiguous=True).then_inc(sem("gains"), 16)
            gains = [(B_SBQ, "sb_q_gain"), (B_SBK, "sb_k_gain"), (B_RQ, "ret_q_gain"), (B_RK, "ret_k_gain"),
                     (B_Q2, "q_norm_2"), (B_K2, "k_norm_2"), (B_GG, "ret_gn_gain"), (B_GB, "ret_gn_bias"),
                     (B_RT, "b_router"), (B_DTB, "dt_bias_f_2"), (B_DTB + SSDH, "dt_bias_b_2"),
                     (B_ALOG, "a_log_f_2"), (B_ALOG + SSDH, "a_log_b_2"), (B_DSK, "d_skip_2")]
            for at, name in gains:
                n = a[name].shape[1]
                act.dma_start(bc[:, at:at + n], a[name].to_broadcast([P, n])).then_inc(sem("gains"), 16)

            def norm(i, src=X):
                for tb in range(NTB):
                    link(nc.scalar.activation(XN[:, tb * D:(tb + 1) * D], src[:, tb * D:(tb + 1) * D], ACT.Square,
                                              accum_out=stat[:, tb:tb + 1]))
                nc.scalar.activation(stat[:, 2:4], stat[:, 0:2], ACT.Sqrt, scale=1.0 / D, bias=eps).then_inc(sem("rms"), 1)

            def norm_evac(i, gain):
                for b in (1, 3):
                    act.wait_ge(sem("xnT_ps"), 4 * i + b + 1)
                    for c in (2 * b, 2 * b + 1):
                        ins = nc.scalar.activation(XNT[:, c * 256:(c + 1) * 256], PS[:, 4 + b, (c % 2) * 256:(c % 2) * 256 + 256],
                                                   ACT.Copy, scale=vecT[:, gain + c:gain + c + 1])
                    ins.then_inc(sem("xnT_act"), 1)

            def head_sd(i, n):
                act.wait_ge(sem("head_sq"), i)
                nc.scalar.activation(stat[:, 32:32 + n], stat[:, 8:8 + n], ACT.Sqrt, scale=1.0 / HD, bias=eps).then_inc(sem("head_sd"), 1)

            def group_out(g):
                act.wait_ge(sem("w_used"), place[("in", g, 1)] + 1)
                nc.scalar.activation(PR[g], banks(2 * (g % 2), 2), ACT.Copy).then_inc(sem("proj_sb"), 1)

            act.wait_ge(sem("consts"), 16)
            act.wait_ge(sem("x_in"), 16)
            norm(0)
            act.wait_ge(sem("vecT"), 1)
            norm_evac(0, V_MIX)
            act.wait_ge(sem("trig_r"), 1)
            nc.scalar.activation(rope[:, 64:128], TMP[:, 0:64], ACT.Sin).then_inc(sem("trig"), 1)
            nc.scalar.activation(rope[:, 0:64], TMP[:, 0:64], ACT.Sin, scale=0.5).then_inc(sem("trig"), 1)
            group_out(0)
            group_out(1)
            head_sd(1, 16)
            group_out(2)
            head_sd(2, 16)
            z = PS[:, 4:6, 0:384]
            for b in range(4):
                act.wait_ge(sem("sb_z"), b + 1)
                t0 = t3(SBT[0], 2)
                nc.scalar.activation(t0, z, ACT.Abs, scale=HD ** -0.5).then_inc(sem("sb_a"), 1)
                act.wait_ge(sem("sb_a"), b + 1)
                link(nc.scalar.activation(t0, t0, ACT.Exp, scale=-1.0))
                nc.scalar.activation(t0, t0, ACT.Ln, bias=1.0).then_inc(sem("sb_l"), 1)
                act.wait_ge(sem("sb_t"), b + 1)
                nc.scalar.activation(SBT[3], SBT[3], ACT.Exp).then_inc(sem("sb_e"), 1)
                group_out(3 + b)
                act.wait_ge(sem("sb_pv"), b + 1)
                nc.scalar.activation(YT[:, b * 256:(b + 1) * 256], PS[:, 4, 0:256], ACT.Copy).then_inc(sem("yt"), 1)
            act.wait_ge(sem("proj_sb"), NSEG)
            nc.scalar.activation(PR[6], PR[6], ACT.Silu).then_inc(sem("silu_g"), 1)
            head_sd(3, 16)
            head_sd(4, 16)
            head_sd(5, 16)
            act.wait_ge(sem("ybT_ps"), 1)
            nc.scalar.activation(YT[:, 1024:2048], banks(6, 2), ACT.Copy).then_inc(sem("ybT"), 1)

            act.wait_ge(sem("x1"), 1)
            act.dma_start(BUP, a["b_up_gate"][0]).then_inc(sem("late_in"), 16)
            act.dma_start(BDN, a["b_down"][0]).then_inc(sem("late_in"), 16)
            act.dma_start(t3(PIN, 2), a["p"][0][0].rearrange("(b p) d -> p b d", p=P)).then_inc(sem("late_in"), 16)
            norm(1)
            norm_evac(1, V_FFN)
            act.wait_ge(sem("neg_max"), 1)
            for tb in range(NTB):
                nc.scalar.activation(EXM[:, tb * E:(tb + 1) * E], logit[:, tb * E:(tb + 1) * E], ACT.Exp,
                                     bias=stat[:, 4 + tb:5 + tb]).then_inc(sem("ex"), 1)
            act.wait_ge(sem("gT_ps"), 1)
            nc.scalar.activation(GTT, PS[0:E, 2, 0:256], ACT.Copy).then_inc(sem("gT"), 1)

            def sigmoid(sig_in, sig_out, value):
                act.wait_ge(sem(sig_in), value)
                nc.scalar.activation(SIG, GLU, ACT.Sigmoid, scale=1.702).then_inc(sem(sig_out), 1)

            with act.Fori(0, n_experts) as e:
                sigmoid("glu", "sig", e + 1)
                act.wait_ge(sem("spread"), e + 1)
                nc.scalar.activation(SPT, PS[:, 7, 0:256], ACT.Copy).then_inc(sem("sT_slots"), 1)
                act.wait_ge(sem("hT_ps"), e + 1)
                nc.scalar.activation(HTS, PS[:, 6, :], ACT.Copy).then_inc(sem("hT"), 1)
            act.wait_ge(sem("flags"), 1)
            any_more = act.value_load(flag_i[0:1, 96:97])
            with act.If(any_more > 0):
                with act.Fori(0, PASSES - 1) as p:
                    with act.Fori(0, E) as e:
                        more = act.value_load(flag_i[0:1, bass.ds(p * E + e, 1)])
                        with act.If(more > 0):
                            t = p * E + e
                            act.wait_ge(sem("ov_gathered"), t * 2 + 2)
                            nc.scalar.activation(SPT, PS[:, 7, 0:256], ACT.Copy).then_inc(sem("sT_slots"), 1)
                            act.wait_ge(sem("sT_slots"), t + (n_experts + 1))
                            sigmoid("ov_glu", "ov_sig", t + 1)
                            act.wait_ge(sem("ov_hT_ps"), t + 1)
                            nc.scalar.activation(HTS, PS[:, 6, :], ACT.Copy).then_inc(sem("ov_hT"), 1)
                            act.wait_ge(sem("ov_hT"), t + 1)
                            act.sem_inc(sem("pass_end"), 1)
                        with act.Else():
                            act.sem_inc(sem("sT_slots"), 1)
                            act.sem_inc(sem("ov_sig"), 1)
                            act.sem_inc(sem("ov_hT"), 1)
                        act.nop()
                act.nop()
            with act.Else():
                act.nop()
            act.nop()

            act.wait_ge(sem("pT_ps"), 1)
            nc.scalar.activation(PT, PS[:, 6, :], ACT.Copy).then_inc(sem("pT"), 1)
            act.wait_ge(sem("x2"), 1)
            act.dma_start(N1P, a["norm1_post_2"].to_broadcast([P, D])).then_inc(sem("late_in"), 16)
            norm(2)
            norm_evac(2, V_PLE)
            act.wait_ge(sem("w_used"), place[("ple_gate", 1, 1)] + 1)
            nc.scalar.activation(SG, banks(0, 4), ACT.Sigmoid).then_inc(sem("ple_gate"), 1)
            act.wait_ge(sem("x3"), 1)
            norm(3)
            norm_evac(3, V_N1)
            for c in range(6):
                act.wait_ge(sem("w_used"), place[("xbc", c)] + 1)
                nc.scalar.activation(UB[:, 2 * c:2 * c + 2, 2:258], PS[:, c, :].rearrange("p (c n) -> p c n", c=2),
                                     ACT.Copy).then_inc(sem("xbc_sb"), 1)
            act.wait_ge(sem("dt_abs"), 1)
            link(nc.scalar.activation(DTA, DT, ACT.Abs))
            link(nc.scalar.activation(DTA, DTA, ACT.Exp, scale=-1.0))
            nc.scalar.activation(DTA, DTA, ACT.Ln, bias=1.0).then_inc(sem("a_exp"), 1)
            nc.scalar.activation(AEX, bc[:, B_ALOG:B_ALOG + 32], ACT.Exp).then_inc(sem("a_exp"), 1)
            act.wait_ge(sem("w_used"), place["kv"] + 1)
            kv = PS[:, 7, :].rearrange("p (b n) -> p b n", b=2)
            link(nc.scalar.activation(t3(QK, 2)[:, :, 512:640], kv[:, :, 0:P], ACT.Copy))
            nc.scalar.activation(t3(VV, 2), kv[:, :, P:256], ACT.Copy).then_inc(sem("kv_sb"), 1)
            act.wait_ge(sem("w_used"), place[("q", 0, 1)] + 1)
            nc.scalar.activation(t3(QK, 2)[:, :, 0:512], PS[:, 0:2, :], ACT.Copy).then_inc(sem("q_sb"), 1)
            head_sd(6, 20)

            silus = iter(range(CC))

            def conv_silu(n):
                for _ in range(n):
                    c = next(silus)
                    act.wait_ge(sem("conv"), c + 1)
                    nc.scalar.activation(XBT[:, c, :], XBT[:, c, :], ACT.Silu).then_inc(sem("silu_c"), 1)

            gates4 = GATES.rearrange("p (b n) -> p b n", b=2)
            for u in range(4):
                act.wait_ge(sem("s_max"), u + 1)
                for i in range(4):
                    at = 60 + 4 * u + 2 * (i % 2) + i // 2
                    nc.scalar.activation(t3(PE_, 4)[:, i, :], PS[:, i % 2, (i // 2) * 256:(i // 2) * 256 + 256], ACT.Exp,
                                         scale=HD ** -0.5, bias=stat[:, at:at + 1],
                                         accum_out=stat[:, 80 + 4 * u + i:81 + 4 * u + i]).then_inc(sem("p_exp"), 1)
                act.wait_ge(sem("pT2_ps"), u + 1)
                nc.scalar.activation(PTS, banks(2, 2), ACT.Copy).then_inc(sem("pT2"), 1)
                act.wait_ge(sem("w_used"), place[("gates", u, 1)] + 1)
                nc.scalar.activation(gates4[:, :, u * 512:(u + 1) * 512], PS[:, 6:8, :], ACT.Sigmoid).then_inc(sem("gate2"), 1)
            conv_silu(CC)
            act.wait_ge(sem("attT_ps"), 1)
            nc.scalar.activation(ATTT, banks(4, 2), ACT.Copy).then_inc(sem("attT"), 1)
            act.wait_ge(sem("xs_ps"), 1)
            nc.scalar.activation(XS, banks(0, 4), ACT.Copy).then_inc(sem("xs"), 1)
            z4 = t3(Z, 2)
            for h in range(SSDH):
                act.wait_ge(sem("e_sub"), h + 1)
                nc.scalar.activation(EE[h % 2], EE[h % 2], ACT.Exp).then_inc(sem("e_exp"), 1)
                if h in (6, 12):
                    g = h // 6 - 1
                    act.wait_ge(sem("w_used"), place[("z", g, 1)] + 1)
                    nc.scalar.activation(z4[:, :, g * 512:(g + 1) * 512], PS[:, 6:8, :], ACT.Silu).then_inc(sem("z_sb"), 1)
            act.wait_ge(sem("y_mul"), 1)
            norm(4, XNT)
            norm_evac(4, V_SSD)
            for b in (1, 3):
                act.wait_ge(sem("mixT_ps"), b + 1)
                nc.scalar.activation(XNT[:, b * 512:(b + 1) * 512], PS[:, 4 + b, :], ACT.Copy).then_inc(sem("mixT_act"), 1)
            act.dma_start(N2P, a["norm2_post_2"].to_broadcast([P, D])).then_inc(sem("post2_in"), 16)

            def post_norm(key):
                act.wait_ge(sem("w_used"), place[key] + 1)
                for tb in range(NTB):
                    link(nc.scalar.activation(XN[:, tb * D:(tb + 1) * D], banks(2 * tb, 2), ACT.Square,
                                              accum_out=stat[:, tb:tb + 1]))
                nc.scalar.activation(stat[:, 2:4], stat[:, 0:2], ACT.Sqrt, scale=1.0 / D, bias=eps).then_inc(sem("post_sd"), 1)

            post_norm(("out2", 1, 1))
            act.wait_ge(sem("x4"), 1)
            norm(5)
            norm_evac(5, V_N2)
            for j in range(FC // 2):
                act.wait_ge(sem("w_used"), place[("gate", j)] + 1)
                if j >= 2:
                    act.wait_ge(sem("ffn_act"), j - 1)
                nc.scalar.activation(SF[j % 2], PS[:, 2 * (j % 4), :], ACT.Silu).then_inc(sem("silu_f"), 1)
            post_norm(("ffn_down", FC // 2 - 1))

        @block.vector
        def _(dve):
            link, count = chain(dve, "dve_step")
            V = nc.vector
            tt, ts, stt = V.tensor_tensor, V.tensor_scalar, V.scalar_tensor_tensor

            def norm(i, src=X, dst=XN):
                dve.wait_ge(sem("rms"), i + 1)
                link(V.reciprocal(stat[:, 6:8], stat[:, 2:4]))
                for tb in range(NTB):
                    ts(dst[:, tb * D:(tb + 1) * D], src[:, tb * D:(tb + 1) * D], stat[:, 6 + tb:7 + tb], None, ALU.mult).then_inc(sem("xn"), 1)

            def norm_evac(i, gain):
                for b in (0, 2):
                    dve.wait_ge(sem("xnT_ps"), 4 * i + b + 1)
                    for c in (2 * b, 2 * b + 1):
                        ins = ts(XNT[:, c * 256:(c + 1) * 256], PS[:, 4 + b, (c % 2) * 256:(c % 2) * 256 + 256],
                                 vecT[:, gain + c:gain + c + 1], None, ALU.mult)
                    ins.then_inc(sem("xnT_dve"), 1)
                dve.wait_ge(sem("xnT_ps"), 4 * i + 4)

            n_head = [0]

            def head_norm(src, n, gains, tmp):
                link(tt(tmp, src, src, ALU.mult))
                n_head[0] += 1
                V.reduce_sum(stat[:, 8:8 + n], tmp.rearrange("p (h d) -> p h d", d=HD), AX.X).then_inc(sem("head_sq"), 1)
                dve.wait_ge(sem("head_sd"), n_head[0])
                link(V.reciprocal(stat[:, 8:8 + n], stat[:, 32:32 + n]))
                s3 = src.rearrange("p (h d) -> p h d", d=HD)
                link(tt(s3, s3, spread_last(stat[:, 8:8 + n], HD), ALU.mult))
                return [tt(s, s, g, ALU.mult) for s, g in gains]

            def rotate(x0, x1, cos, sin, tmp):
                t = tmp
                link(tt(t[0], x0, cos, ALU.mult))
                link(tt(t[1], x1, sin, ALU.mult))
                link(tt(t[2], x1, cos, ALU.mult))
                link(tt(t[3], x0, sin, ALU.mult))
                link(tt(x0, t[0], t[1], ALU.subtract))
                return tt(x1, t[2], t[3], ALU.add)

            dve.wait_ge(sem("consts"), 16)
            dve.wait_ge(sem("vecT_ps"), 1)
            V.tensor_copy(vecT[:, :], PS[:, 0, 0:NVEC]).then_inc(sem("vecT"), 1)
            dve.wait_ge(sem("vecT"), 1)
            norm(0)
            norm_evac(0, V_MIX)
            dve.wait_ge(sem("gains"), 15 * 16)
            link(V.tensor_copy(stat[:, 100:102], pos_i[:, :]))
            for tb in range(NTB):
                link(ts(TMP[:, tb * 32:(tb + 1) * 32], cc(C_FRQ, 32), stat[:, 100 + tb:101 + tb], None, ALU.mult))
            ang, turns = TMP[:, 0:64], TMP[:, 64:128]
            link(ts(turns, ang, TWO_PI_INV, ROUND, ALU.mult, ALU.add))
            link(ts(turns, turns, ROUND, None, ALU.subtract))
            for part in (PI2_A, PI2_B, PI2_C):
                link(stt(ang, turns, -part, ang, ALU.mult, ALU.add))
            ts(ang, ang, PI_IN, -PI_IN, ALU.min, ALU.max).then_inc(sem("trig_r"), 1)
            dve.wait_ge(sem("trig"), 2)
            cos, sin = rope[:, 0:64], rope[:, 64:128]
            link(tt(cos, cos, cos, ALU.mult))
            link(ts(cos, cos, -2.0, 1.0, ALU.mult, ALU.add))

            def gain3(at, n):
                return bcast(bc[:, at:at + HD], n)

            def heads(ap):
                return ap.rearrange("p (h d) -> p h d", d=HD)

            def qkT_evac(i, bank):
                dve.wait_ge(sem("qkT_ps"), i + 1)
                V.tensor_copy(QKT[i], banks(bank, 2)).then_inc(sem("qkT"), 1)

            dve.wait_ge(sem("proj_sb"), 1)
            head_norm(PR[0], 16, [(heads(PR[0]), gain3(B_SBQ, 16))], TMP)[0].then_inc(sem("ret_qk"), 1)
            dve.wait_ge(sem("proj_sb"), 2)
            head_norm(PR[1], 16, [(heads(PR[1]), gain3(B_SBK, 16))], TMP)[0].then_inc(sem("ret_qk"), 1)
            qkT_evac(0, 4)
            qkT_evac(1, 6)
            z, tail = PS[:, 4:6, 0:384], PS[:, 6:8, 0:384]
            t0, t1, t2, t3_ = (t3(x, 2) for x in SBT)
            sbm = bcast(cc(C_SBM, 384), 2)
            for b in range(4):
                dve.wait_ge(sem("sb_a"), b + 1)
                link(ts(t1, z, HD ** -0.5, 0.0, ALU.mult, ALU.max))
                dve.wait_ge(sem("sb_l"), b + 1)
                link(tt(t1, t1, t0, ALU.add))
                tt(t2, t1, sbm, ALU.mult).then_inc(sem("sb_m"), 1)
                link(stt(t3_, z, HD ** -0.5, t1, ALU.mult, ALU.subtract))
                dve.wait_ge(sem("sb_tail"), b + 1)
                tt(t3_, t3_, tail, ALU.add).then_inc(sem("sb_t"), 1)
                dve.wait_ge(sem("sb_e"), b + 1)
                stt(t3_, t3_, -1.0, sbm, ALU.mult, ALU.mult).then_inc(sem("sb_w"), 1)
            for s, g in ((3, B_RQ), (4, B_RK)):
                dve.wait_ge(sem("proj_sb"), s + 1)
                link(head_norm(PR[s], 16, [(heads(PR[s]), gain3(g, 16))], TMP)[0])
                for tb in range(NTB):
                    x = PR[s][:, tb * 512:(tb + 1) * 512].rearrange("p (h b d) -> p h b d", h=NH, b=2)
                    c3, s3 = (bcast(v[:, tb * 32:(tb + 1) * 32], NH) for v in (cos, sin))
                    ins = rotate(x[:, :, 0, :], x[:, :, 1, :], c3, s3, [r.rearrange("p (h d) -> p h d", h=NH) for r in ROT])
                    if tb == 0:
                        link(ins)
                ins.then_inc(sem("ret_qk"), 1)
                dve.wait_ge(sem("ret_qk"), s)
            qkT_evac(2, 6)
            qkT_evac(3, 4)
            for h in range(NH):
                dve.wait_ge(sem("ret_s"), h + 1)
                dm = cc(C_DM + h * 256, 256)
                w = WR[:, h * 384:(h + 1) * 384]
                tt(w[:, 0:256], PS[:, h % 4, 0:256], dm, ALU.mult)
                tt(w[:, 256:384], PS[:, h % 4, 256:384], dm[:, 0:P], ALU.mult).then_inc(sem("ret_w"), 1)
            dve.wait_ge(sem("ret_y"), 1)
            y = PS[:, 4:6, :].rearrange("p b (h d) -> p (b h) d", d=HD)
            yb3 = heads(YB)
            link(V.reduce_sum(stat[:, 8:24], y, AX.X))
            link(ts(stat[:, 8:24], stat[:, 8:24], 1.0 / HD, None, ALU.mult))
            link(tt(yb3, y, spread_last(stat[:, 8:24], HD), ALU.subtract))
            link(tt(TMP, YB, YB, ALU.mult))
            n_head[0] += 1
            V.reduce_sum(stat[:, 8:24], heads(TMP), AX.X).then_inc(sem("head_sq"), 1)
            dve.wait_ge(sem("head_sd"), n_head[0])
            link(V.reciprocal(stat[:, 8:24], stat[:, 32:48]))
            link(tt(yb3, yb3, spread_last(stat[:, 8:24], HD), ALU.mult))
            link(tt(t3(YB, 2), t3(YB, 2), bcast(bc[:, B_GG:B_GG + 512], 2), ALU.mult))
            link(tt(t3(YB, 2), t3(YB, 2), bcast(bc[:, B_GB:B_GB + 512], 2), ALU.add))
            dve.wait_ge(sem("silu_g"), 1)
            tt(YB, YB, PR[6], ALU.mult).then_inc(sem("yb"), 1)
            dve.wait_ge(sem("w_used"), place[("out", 1, 1)] + 1)
            tt(X, X, banks(0, 4), ALU.add).then_inc(sem("x1"), 1)
            dve.wait_ge(sem("x1"), 1)
            norm(1)
            norm_evac(1, V_FFN)
            dve.wait_ge(sem("w_used"), place["router"] + 1)
            link(tt(t3(logit, 2), PS[:, 0, 0:64].rearrange("p (b e) -> p b e", b=2), bcast(bc[:, B_RT:B_RT + E], 2), ALU.add))
            for tb in range(NTB):
                lg = logit[:, tb * E:(tb + 1) * E]
                tv = top_v[:, tb * 8:(tb + 1) * 8]
                link(V.max(tv, lg))
                link(V.max_index(top_i[:, tb * 8:(tb + 1) * 8], tv, lg))
                ts(stat[:, 4 + tb:5 + tb], tv[:, 0:1], -1.0, None, ALU.mult).then_inc(sem("neg_max") if tb else sem("dve_step"), 1)
                if tb == 0:
                    count[0] += 1
            idx_f = stat[:, 104:120]
            link(V.tensor_copy(idx_f, top_i[:, :]))
            for tb in range(NTB):
                mk = MASK[:, tb * E:(tb + 1) * E]
                link(ts(mk, cc(C_EXP, E), idx_f[:, tb * 8:tb * 8 + 1], None, ALU.is_equal))
                for k in range(1, TOPK):
                    ins = stt(mk, cc(C_EXP, E), idx_f[:, tb * 8 + k:tb * 8 + k + 1], mk, ALU.is_equal, ALU.add)
                    if tb == 1 and k == TOPK - 1:
                        ins.then_inc(sem("mask"), 1)
                        dve.wait_ge(sem("mask"), 1)
                    else:
                        link(ins)
            dve.wait_ge(sem("ex"), 2)
            link(tt(EXM, EXM, MASK, ALU.mult))
            link(V.reduce_sum(stat[:, 8:10], t3(EXM, 2), AX.X))
            link(V.reciprocal(stat[:, 8:10], stat[:, 8:10]))
            g3, s3 = t3(gate_of[:, :], 2), t3(slot_of[:, :], 2)
            link(V.memset(gate_of[:, :], 0.0))
            tt(g3[:, :, 0:E], t3(EXM, 2), spread_last(stat[:, 8:10], E), ALU.mult).then_inc(sem("gates"), 1)
            dve.wait_ge(sem("pos_ps"), 1)
            link(V.memset(slot_of[:, :], -1.0))
            link(stt(s3[:, :, 0:E], PS[:, 1, 0:64].rearrange("p (b e) -> p b e", b=2), 1.0, t3(MASK, 2), ALU.add, ALU.mult))
            link(ts(s3[:, :, 0:E], s3[:, :, 0:E], 1.0, None, ALU.subtract))
            for p in range(PASSES - 1):
                link(ts(flag_f[0:1, p * E:(p + 1) * E], PS[0:1, 1, 64:96], float(CAP * (p + 1)), None, ALU.is_gt))
            link(V.reduce_max(flag_f[0:1, 96:97], flag_f[0:1, 0:E], AX.X))
            V.tensor_copy(flag_i[0:1, 0:97], flag_f[0:1, 0:97]).then_inc(sem("flags"), 1)
            dve.wait_ge(sem("flags"), 1)
            dve.wait_ge(sem("gates"), 1)

            def one_hot(e, tb, slots, weighted):
                at = bass.ds(e + tb * (E + 1), 1) if not isinstance(e, int) else slice(e + tb * (E + 1), e + tb * (E + 1) + 1)
                if weighted:
                    return ts(OHG[:, tb * P:(tb + 1) * P], slots, slot_of[:, at], gate_of[:, at], ALU.is_equal, ALU.mult)
                return ts(OH[:, tb * P:(tb + 1) * P], slots, slot_of[:, at], None, ALU.is_equal)

            def select(e):
                at = bass.ds(e + C_ID, 1) if not isinstance(e, int) else slice(C_ID + e, C_ID + e + 1)
                return V.tensor_copy(SEL, cst[0:E, at].to_broadcast([E, CAP]))

            gain_cols = spread_last(vecT[:, V_FFN:V_FFN + KC], CAP)

            def gathered_out(sig):
                tt(XG.rearrange("p (c s) -> p c s", c=KC), PS[:, 6, :].rearrange("p (c s) -> p c s", c=KC), gain_cols,
                   ALU.mult).then_inc(sem(sig), 1)

            slots0 = cc(C_SLOT)
            one_hot(0, 0, slots0, False)
            one_hot(0, 1, slots0, False).then_inc(sem("onehot"), 1)
            select(0).then_inc(sem("sel"), 1)
            dve.wait_ge(sem("gathered"), 1)
            gathered_out("x_slots")
            start = count[0]
            with dve.Fori(0, n_experts) as e:
                one_hot(e + 1, 0, slots0, False)
                one_hot(e + 1, 1, slots0, False).then_inc(sem("onehot"), 1)
                one_hot(e, 0, slots0, True)
                one_hot(e, 1, slots0, True).then_inc(sem("weighted"), 1)
                dve.wait_ge(sem("w_used"), e * PER_EXPERT + (before_experts + KC))
                ts(GLU, PS[:, 4, :], 7.0, None, ALU.min).then_inc(sem("glu"), 1)
                ts(LIN, PS[:, 5, :], 7.0, -7.0, ALU.min, ALU.max).then_inc(sem("dve_step"), 1)
                dve.wait_ge(sem("dve_step"), e * 2 + (start + 1))
                stt(LIN, LIN, 1.0, GLU, ALU.add, ALU.mult).then_inc(sem("dve_step"), 1)
                dve.wait_ge(sem("dve_step"), e * 2 + (start + 2))
                dve.wait_ge(sem("sig"), e + 1)
                tt(HH, LIN, SIG, ALU.mult).then_inc(sem("h_done"), 1)
                select(e + 1).then_inc(sem("sel"), 1)
                dve.wait_ge(sem("gathered"), e + 2)
                gathered_out("x_slots")
                dve.wait_ge(sem("w_used"), e * PER_EXPERT + (before_experts + PER_EXPERT))
                V.tensor_copy(YS, PS[:, 7, :]).then_inc(sem("y_slots"), 1)
            count[0] = start + 2 * n_experts
            dve.wait_ge(sem("scattered"), n_experts)
            any_more = dve.value_load(flag_i[0:1, 96:97])
            start = count[0]
            with dve.If(any_more > 0):
                with dve.Fori(0, PASSES - 1) as p:
                    with dve.Fori(0, E) as e:
                        more = dve.value_load(flag_i[0:1, bass.ds(p * E + e, 1)])
                        with dve.If(more > 0):
                            t = p * E + e
                            dve.wait_ge(sem("scattered"), t + n_experts)
                            slots = cst[:, bass.ds(p * P + (C_SLOT + P), P)]
                            one_hot(e, 0, slots, False)
                            one_hot(e, 1, slots, False)
                            one_hot(e, 0, slots, True)
                            one_hot(e, 1, slots, True)
                            select(e).then_inc(sem("ov_onehot"), 1)
                            dve.wait_ge(sem("ov_gathered"), t * 2 + 2)
                            gathered_out("ov_x")
                            dve.wait_ge(sem("w_used"), t * PER_EXPERT + (before_experts + KC + PER_EXPERT * E))
                            ts(GLU, PS[:, 4, :], 7.0, None, ALU.min).then_inc(sem("ov_glu"), 1)
                            ts(LIN, PS[:, 5, :], 7.0, -7.0, ALU.min, ALU.max).then_inc(sem("dve_step"), 1)
                            dve.wait_ge(sem("dve_step"), t * 2 + (start + 1))
                            stt(LIN, LIN, 1.0, GLU, ALU.add, ALU.mult).then_inc(sem("dve_step"), 1)
                            dve.wait_ge(sem("dve_step"), t * 2 + (start + 2))
                            dve.wait_ge(sem("ov_sig"), t + 1)
                            tt(HH, LIN, SIG, ALU.mult).then_inc(sem("ov_h"), 1)
                            dve.wait_ge(sem("w_used"), t * PER_EXPERT + (before_experts + PER_EXPERT * (E + 1)))
                            V.tensor_copy(YS, PS[:, 7, :]).then_inc(sem("ov_y"), 1)
                            dve.wait_ge(sem("ov_y"), t + 1)
                            dve.sem_inc(sem("pass_end"), 1)
                        with dve.Else():
                            for s in ("ov_onehot", "ov_x", "ov_glu", "ov_h", "ov_y"):
                                dve.sem_inc(sem(s), 1)
                            dve.sem_inc(sem("dve_step"), 2)
                        dve.nop()
                dve.nop()
            with dve.Else():
                dve.sem_inc(sem("dve_step"), 2 * (PASSES - 1) * E)
            count[0] = start + 2 * (PASSES - 1) * E
            dve.wait_ge(sem("scattered"), n_experts + (PASSES - 1) * E)
            tt(X, X, banks(0, 4), ALU.add).then_inc(sem("x2"), 1)
            dve.wait_ge(sem("x2"), 1)
            norm(2)
            norm_evac(2, V_PLE)
            dve.wait_ge(sem("w_used"), place["ple_proj"] + 1)
            dve.wait_ge(sem("ple_gate"), 1)
            link(tt(SG, SG, banks(4, 4), ALU.mult))
            tt(X, X, SG, ALU.add).then_inc(sem("x3"), 1)
            dve.wait_ge(sem("x3"), 1)
            link(V.memset(UB[:, :, 0:2], 0.0))
            link(V.memset(UB[:, :, 258:260], 0.0))
            norm(3)
            norm_evac(3, V_N1)

            def conv(c):
                dve.wait_ge(sem("xbc_sb"), c // 2 + 1)
                link(ts(XBT[:, c, :], UB[:, c, 0:256], vecT[:, V_CW + c:V_CW + c + 1], vecT[:, V_CB + c:V_CB + c + 1], ALU.mult, ALU.add))
                for k in range(1, CONVK):
                    w = vecT[:, V_CW + k * CC + c:V_CW + k * CC + c + 1]
                    ins = stt(XBT[:, c, :], UB[:, c, k:k + 256], w, XBT[:, c, :], ALU.mult, ALU.add)
                    if k < CONVK - 1:
                        link(ins)
                ins.then_inc(sem("conv"), 1)

            for c in range(CC):
                conv(c)
            dve.wait_ge(sem("w_used"), place["dt"] + 1)
            tt(t3(DT, 2), PS[:, 6, 0:64].rearrange("p (b n) -> p b n", b=2), bcast(bc[:, B_DTB:B_DTB + 32], 2), ALU.add).then_inc(sem("dt_abs"), 1)
            dve.wait_ge(sem("dt_abs"), 1)
            dve.wait_ge(sem("a_exp"), 2)
            stt(DT, DT, 0.0, DTA, ALU.max, ALU.add).then_inc(sem("dt_sp"), 1)
            dve.wait_ge(sem("dt_sp"), 1)
            stt(t3(ADT, 2), t3(DT, 2), -1.0, bcast(AEX, 2), ALU.mult, ALU.mult).then_inc(sem("adt"), 1)
            dve.wait_ge(sem("kv_sb"), 1)
            dve.wait_ge(sem("q_sb"), 1)
            qk4 = QK.rearrange("p (b h d) -> p b h d", b=2, d=HD)
            parts = []
            for tb in range(NTB):
                parts += [(qk4[:, tb, 0:8, :], gain3(B_Q2, 8)), (qk4[:, tb, 8:10, :], gain3(B_K2, 2))]
            for ins in [head_norm(QK, 20, parts, SQ2)][0][-1:]:
                link(ins)
            for tb in range(NTB):
                for i in range(2):
                    x = qk4[:, tb, :, 32 * i:32 * i + 32]
                    at = tb * 32 + 16 * i
                    link(rotate(x[:, :, 0:16], x[:, :, 16:32], bcast(cc(C_COS + at, 16), 10), bcast(cc(C_SIN + at, 16), 10),
                                [r[:, 0:160].rearrange("p (h d) -> p h d", h=10) for r in ROT2]))
            kd = KD.rearrange("p (b h c d) -> p b h c d", b=2, h=2, c=2)
            for tb in range(NTB):
                for c in range(2):
                    ins = V.tensor_copy(kd[:, tb, :, c, :], qk4[:, tb, 8:10, :])
                    if (tb, c) != (1, 1):
                        link(ins)
            ins.then_inc(sem("qk2"), 2)
            dve.wait_ge(sem("qk2T_ps"), 1)
            V.tensor_copy(QT, banks(6, 2)).then_inc(sem("qk2T"), 1)
            dve.wait_ge(sem("qk2T_ps"), 2)
            V.tensor_copy(KT, PS[:, 2, :]).then_inc(sem("qk2T"), 1)
            for u in range(4):
                dve.wait_ge(sem("s_ps"), u + 1)
                link(V.reduce_max(stat[:, 102:106], PS[:, 0:2, :].rearrange("p b (i n) -> p (b i) n", i=2), AX.X))
                ts(stat[:, 60 + 4 * u:64 + 4 * u], stat[:, 102:106], -(HD ** -0.5), None, ALU.mult).then_inc(sem("s_max"), 1)
            dve.wait_ge(sem("p_exp"), 16)
            link(V.reciprocal(stat[:, 80:96], stat[:, 80:96]))
            dve.wait_ge(sem("o_ps"), 4)
            tt(heads(ATT), PS[:, 4:6, :].rearrange("p b (h d) -> p (b h) d", d=HD), spread_last(stat[:, 80:96], HD), ALU.mult).then_inc(sem("att"), 1)
            dve.wait_ge(sem("cb_ps"), 1)
            for g in range(2):
                cbm = CBM[:, g * 768:(g + 1) * 768]
                ps = PS[:, 6 + g, :]
                link(tt(cbm[:, 0:128], ps[:, 0:128], cc(C_LE), ALU.mult))
                link(V.tensor_copy(cbm[:, 128:256], ps[:, 128:256]))
                link(tt(cbm[:, 256:384], ps[:, 384:512], cc(C_LE), ALU.mult))
                link(tt(cbm[:, 384:512], ps[:, 0:128], cc(C_GE), ALU.mult))
                link(tt(cbm[:, 512:640], ps[:, 384:512], cc(C_GE), ALU.mult))
                ins = V.tensor_copy(cbm[:, 640:768], ps[:, 256:384])
                if g == 0:
                    link(ins)
            ins.then_inc(sem("cb"), 1)
            dve.wait_ge(sem("cb"), 1)
            dve.wait_ge(sem("cum_ps"), 1)
            link(V.tensor_copy(CUM, PS[:, 4, 0:64]))
            tt(CUMX, CUM, PS[:, 4, 64:128], ALU.subtract).then_inc(sem("cum_done"), 1)
            dve.wait_ge(sem("cum_done"), 1)
            cum, cumx, dt = t3(CUM, 2), t3(CUMX, 2), t3(DT, 2)

            def exponents(h):
                dve.wait_ge(sem("abc"), h + 1)
                ps, ex = PS[:, 4 + h % 2, :], EE[h % 2]
                f, b = slice(h, h + 1), slice(16 + h, 17 + h)
                rows = ((0, 0, cum[:, 0, f]), (1, 1, cumx[:, 0, f]), (2, 1, cum[:, 1, f]),
                        (3, 2, cum[:, 0, b]), (4, 3, cum[:, 1, b]), (5, 2, cumx[:, 1, b]))
                for blk, src, by in rows:
                    ins = ts(ex[:, blk * P:(blk + 1) * P], ps[:, src * P:(src + 1) * P], by, 0.0, ALU.subtract, ALU.min)
                ins.then_inc(sem("e_sub"), 1)

            def weights(h):
                dve.wait_ge(sem("e_exp"), h + 1)
                if h >= 2:
                    dve.wait_ge(sem("y_ssd"), h - 1)
                ex, w, cbm = EE[h % 2], WW[h % 2], CBM[:, (h // 8) * 768:(h // 8 + 1) * 768]
                f, b = slice(h, h + 1), slice(16 + h, 17 + h)
                for c0, c1, by in ((0, 256, dt[:, 0, f]), (256, 384, dt[:, 1, f]), (384, 512, dt[:, 0, b]), (512, 768, dt[:, 1, b])):
                    ins = stt(w[:, c0:c1], ex[:, c0:c1], by, cbm[:, c0:c1], ALU.mult, ALU.mult)
                ins.then_inc(sem("w_ssd"), 1)
                dve.wait_ge(sem("w_ssd"), h + 1)

            exponents(0)
            for h in range(SSDH):
                if h + 1 < SSDH:
                    exponents(h + 1)
                weights(h)
            Y = XNT
            dve.wait_ge(sem("xs"), 1)
            dve.wait_ge(sem("z_sb"), 2)
            for tb in range(NTB):
                link(tt(Y[:, tb * D:(tb + 1) * D].rearrange("p (h d) -> p h d", d=HD),
                        XS[:, tb * D:(tb + 1) * D].rearrange("p (h d) -> p h d", d=HD),
                        spread_last(bc[:, B_DSK:B_DSK + SSDH], HD), ALU.mult))
            dve.wait_ge(sem("y_ssd"), SSDH)
            link(tt(Y, Y, banks(0, 4), ALU.add))
            tt(Y, Y, Z, ALU.mult).then_inc(sem("y_mul"), 1)
            norm(4, Y)
            norm_evac(4, V_SSD)
            g4 = GATES.rearrange("p (b n) -> p b n", b=2)
            dve.wait_ge(sem("w_used"), place[("attn_proj", 1)] + 1)
            link(tt(t3(M1, 2), banks(4, 4).rearrange("p (b n) -> p b n", b=2), g4[:, :, 0:D], ALU.mult))
            link(tt(t3(XN, 2), banks(0, 4).rearrange("p (b n) -> p b n", b=2), g4[:, :, D:2 * D], ALU.mult))
            tt(XN, XN, M1, ALU.add).then_inc(sem("mixed"), 1)
            for b in (0, 2):
                dve.wait_ge(sem("mixT_ps"), b + 1)
                V.tensor_copy(XNT[:, b * 512:(b + 1) * 512], PS[:, 4 + b, :]).then_inc(sem("mixT_dve"), 1)

            def post_norm(i, gain, signal):
                dve.wait_ge(sem("post_sd"), i + 1)
                link(V.reciprocal(stat[:, 6:8], stat[:, 2:4]))
                for tb in range(NTB):
                    half = XN[:, tb * D:(tb + 1) * D]
                    link(stt(half, banks(2 * tb, 2), stat[:, 6 + tb:7 + tb], gain, ALU.mult, ALU.mult))
                    x = X[:, tb * D:(tb + 1) * D]
                    ins = tt(x, x, half, ALU.add)
                    if signal == "x4" and tb == 0:
                        link(ins)
                    else:
                        ins.then_inc(sem(signal), 1)

            dve.wait_ge(sem("late_in"), 64)
            post_norm(0, N1P, "x4")
            dve.wait_ge(sem("x4"), 1)
            norm(5)
            norm_evac(5, V_N2)
            for j in range(FC // 2):
                dve.wait_ge(sem("w_used"), place[("up", j)] + 1)
                dve.wait_ge(sem("silu_f"), j + 1)
                tt(ACTT[:, 2 * j:2 * j + 2, :].rearrange("p f t -> p (f t)"), SF[j % 2], PS[:, 2 * (j % 4) + 1, :], ALU.mult).then_inc(sem("ffn_act"), 1)
            dve.wait_ge(sem("post2_in"), 16)
            post_norm(1, N2P, "done")



_INS = ["x", "p", "positions", "g_mix_norm", "w_in", "sb_q_gain", "sb_k_gain", "ret_q_gain", "ret_k_gain",
        "ret_gn_gain", "ret_gn_bias", "w_out", "g_ffn_norm", "w_router", "b_router", "w_up_gate", "b_up_gate",
        "w_down", "b_down", "g_ple_norm", "w_ple_gate", "w_ple_proj", "w_in_2", "q_norm_2", "k_norm_2", "conv_w_2",
        "conv_b_2", "dt_bias_f_2", "dt_bias_b_2", "a_log_f_2", "a_log_b_2", "d_skip_2", "ssd_norm_2",
        "w_attn_proj_2", "w_ssd_proj_2", "w_out_2", "norm1_pre_2", "norm1_post_2", "norm2_pre_2", "norm2_post_2",
        "w_gate_up_2", "w_down_2"]


def kernel(**inputs):
    import concourse.bacc as _bacc
    from concourse.bass_utils import run_bass_kernel_spmd as _run

    nc = _bacc.Bacc("TRN2", target_bir_lowering=False, num_devices=1)
    arrays, aps = {}, {}
    for name in _INS:
        arr = np.ascontiguousarray(inputs[name])
        arrays[f"in_{name}"] = arr
        aps[name] = nc.dram_tensor(f"in_{name}", arr.shape, mybir.dt.from_np(arr.dtype), kind="ExternalInput").ap()
    arrays["consts"] = constants()
    aps["consts"] = nc.dram_tensor("consts", (P, NCONST), F32, kind="ExternalInput").ap()
    out = nc.dram_tensor("out", (1, T, D), F32, kind="ExternalOutput").ap()
    build_program(nc, aps, out)
    r = _run(nc, [arrays], core_ids=[0])
    return r.results[0]["out"]
```

```python
from contextlib import ExitStack

import numpy as np

import concourse.bass as bass
from concourse import mybir

F32 = mybir.dt.float32
F32R = mybir.dt.float32r
I32 = mybir.dt.int32
U32 = mybir.dt.uint32
ALU = mybir.AluOpType
ACT = mybir.ActivationFunctionType
AX = mybir.AxisListType

P = 128
T = 256
NTB = T // P
D = 1024
KC = D // P
HD = 64
NH = 8
NSEG = 7
SEG_ORDER = (0, 1, 3, 2, 4, 5, 6)
E = 32
TOPK = 4
CAP = 64
PASSES = T // CAP
DFF = 2816
FC = DFF // P
EPS = 1e-6
SLOT = 2048
RING = 12
RAW = 6
BUF = 3
EXPERT_SLOT = (1, 2, 3, 4, 5, 0, 6, 7, 8, 9, 10, 11)
PER_EXPERT = 12
CONVK = 5
CC = 12
SSDH = 16

C_ID = 0
C_EPS = P
C_EARLY = P + 2
C_LE, C_GE, C_LT, C_GT, C_ONE = (C_EARLY + i * P for i in range(5))
C_SBM = C_EARLY + 5 * P
C_DM = C_SBM + 3 * P
C_SLOT = C_DM + NH * 2 * P
C_EXP = C_SLOT + PASSES * P
C_FRQ = C_EXP + E
C_COS = C_FRQ + HD // 2
C_SIN = C_COS + 2 * 32
NCONST = C_SIN + 2 * 32

V_MIX, V_FFN, V_PLE, V_SSD, V_N1, V_N2 = (i * KC for i in range(6))
V_CW = 6 * KC
V_CB = V_CW + CONVK * CC
NVEC = V_CB + CC

B_SBQ, B_SBK, B_RQ, B_RK, B_Q2, B_K2 = (i * HD for i in range(6))
B_GG = 6 * HD
B_GB = B_GG + 512
B_RT = B_GB + 512
B_DTB = B_RT + E
B_ALOG = B_DTB + 2 * SSDH
B_DSK = B_ALOG + 2 * SSDH
NBC = B_DSK + SSDH

TWO_PI_INV = float(1.0 / (2 * np.pi))
PI2_A = 6.28125
PI2_B = float(np.float32(2 * np.pi - PI2_A))
PI2_C = float(2 * np.pi - PI2_A - np.float64(np.float32(2 * np.pi - PI2_A)))
ROUND = 12582912.0
PI_IN = 3.1415925


def constants():
    c = np.zeros((P, NCONST), np.float32)
    i = np.arange(P)
    row, col = i[:, None], i[None, :]
    c[:, C_ID:C_ID + P] = row == col
    c[:, C_LE:C_LE + P] = row <= col
    c[:, C_GE:C_GE + P] = row >= col
    c[:, C_LT:C_LT + P] = row < col
    c[:, C_GT:C_GT + P] = row > col
    c[:, C_ONE:C_ONE + P] = 1.0
    c[:, C_SBM:C_SBM + P] = -(row < col).astype(np.float32)
    c[:, C_SBM + P:C_SBM + 2 * P] = -1.0
    c[:, C_SBM + 2 * P:C_SBM + 3 * P] = -(row < col).astype(np.float32)
    log_g = np.log(1.0 - 2.0 ** (-5.0 - np.arange(NH)))
    for h in range(NH):
        at = C_DM + h * 2 * P
        diff = (col - row).astype(np.float64)
        c[:, at:at + P] = np.where(diff >= 0, np.exp(log_g[h] * np.maximum(diff, 0)), 0) * HD ** -0.5
        c[:, at + P:at + 2 * P] = np.exp(log_g[h] * (diff + P)) * HD ** -0.5
    for p in range(PASSES):
        c[:, C_SLOT + p * P:C_SLOT + (p + 1) * P] = CAP * p + col % CAP
    c[:, C_EXP:C_EXP + E] = np.arange(E)
    half = HD // 2
    c[:, C_FRQ:C_FRQ + half] = np.float32(10000.0) ** (-np.arange(half, dtype=np.float32) / half)
    inv = np.float32(10000.0) ** (-np.arange(0, half, 2, dtype=np.float32) / np.float32(half))
    for tb in range(NTB):
        t = tb * P + i
        ang = np.concatenate([(t // 64)[:, None].astype(np.float32) * inv, (t % 64)[:, None].astype(np.float32) * inv], 1)
        c[:, C_COS + tb * 32:C_COS + (tb + 1) * 32] = np.cos(ang)
        c[:, C_SIN + tb * 32:C_SIN + (tb + 1) * 32] = np.sin(ang)
    c[:, C_EPS:C_EARLY] = EPS
    return c


def build_program(nc, a, out, n_experts=E):
    w_in, w_out, w_up, w_down_e = a["w_in"][0], a["w_out"][0], a["w_up_gate"][0], a["w_down"][0]
    w_in2 = a["w_in_2"][0]

    pieces, number = [], {}

    def piece(name, src, chunks, width):
        number[name] = len(pieces)
        pieces.append((src.rearrange("(k p) n -> p k n", p=P), chunks, width))

    def column_groups(tag, w, col0, groups):
        for g in range(groups):
            for half in range(2):
                piece((tag, g, half), w[half * 512:(half + 1) * 512, col0 + g * 512:col0 + (g + 1) * 512], 4, 512)

    for g in SEG_ORDER:
        for half in range(2):
            piece(("in", g, half), w_in[half * 512:(half + 1) * 512, g * 512:(g + 1) * 512], 4, 512)
    for half in range(2):
        for g in range(2):
            piece(("out", g, half), w_out[half * 512:(half + 1) * 512, g * 512:(g + 1) * 512], 4, 512)
    piece("router", a["w_router"][0], KC, E)
    before_experts = len(pieces)
    ROUNDS = E + (PASSES - 1) * E
    number_of = {}
    base_c = before_experts + PER_EXPERT * ROUNDS
    late = len(pieces)
    column_groups("ple_gate", a["w_ple_gate"][0], 0, 2)
    piece("ple_proj", a["w_ple_proj"][0], 2, D)
    column_groups("q", w_in2, 0, 1)
    piece("kv", w_in2[:, 512:768], KC, 256)
    piece("dt", w_in2[:, 3328:3360], KC, 32)
    for c in range(6):
        piece(("xbc", c), w_in2[:, 1792 + 256 * c:2048 + 256 * c], KC, 256)
    column_groups("gates", w_in2, 3360, 4)
    column_groups("z", w_in2, 768, 2)
    for g in range(2):
        piece(("attn_proj", g), a["w_attn_proj_2"][0][:, g * 512:(g + 1) * 512], 4, 512)
    column_groups("ssd_proj", a["w_ssd_proj_2"][0], 0, 2)
    column_groups("out2", a["w_out_2"][0], 0, 2)
    w_gu = a["w_gate_up_2"][0]
    for j in range(FC // 2):
        piece(("gate", j), w_gu[:, 256 * j:256 * (j + 1)], KC, 256)
        piece(("up", j), w_gu[:, DFF + 256 * j:DFF + 256 * (j + 1)], KC, 256)
    for j in range(FC // 2):
        piece(("ffn_down", j), a["w_down_2"][0][256 * j:256 * (j + 1), :], 2, D)
    place = {k: n if n < late else n - late + base_c for k, n in number.items()}
    keys = sorted(number, key=number.get)

    def raw_slot(key):
        return number[key] % RAW

    def landed_by(key):
        s = raw_slot(key)
        before = sum(1 for k in keys if raw_slot(k) == s and number[k] <= number[key])
        return 16 * (before + (ROUNDS if number[key] >= late else 0))

    def slot_fills(s):
        return sum(1 for k in keys if number[k] < late and raw_slot(k) == s) if s < RAW else 0

    with ExitStack() as ctx:
        def sb(name, cols, dt=F32, parts=P):
            return ctx.enter_context(nc.sbuf_tensor(name, [parts, cols], dt))

        sems = {}

        def sem(name):
            return sems[name]

        names = ("consts consts_late vecs gains x_in late_in post2_in w_used dve_step act_step vecT_ps vecT "
                 "rms_sum rms xn xnT_ps xnT_high xnT w_high w_low yt_high ybT_high pT_high attT_high attn_out first_rows sb_z_read proj_sb head_sq head_sd "
                 "qkT_ps qkT sb_z sb_a sb_l sb_m sb_tail sb_t sb_e sb_w sb_pv yt trig_r trig "
                 "ret_qk ret_s ret_w ret_y silu_g yb ybT_ps ybT x1 "
                 "logitT logit_ps neg_max ex mask pos_ps flags gates gT_ps gT acc0 "
                 "onehot weighted sel gathered spread x_slots glu sig h_done hT_ps hT sT_slots y_slots scattered "
                 "ov_onehot ov_gathered ov_x ov_glu ov_sig ov_h ov_hT_ps ov_hT ov_y pass_end "
                 "x2 pT_ps pT ple_gate x3 xbc_sb dtT dt_ps dt_abs dt_sp a_exp adt cum_ps cum_done kv_sb q_sb conv silu_c "
                 "qk2 qk2T_ps qk2T s_ps s_max p_exp pT2_ps pT2 o_ps att attT_ps attT gate2 "
                 "xs_ps xs cb_ps cb z_sb abc e_sub e_exp w_ssd y_ssd y_mul ssd_xn mixed mixT_ps mixT_high mixT post1_in "
                 "post_sd x4 silu_f ffn_act out_stored done").split()
        for n in names:
            sems[n] = ctx.enter_context(nc.semaphore(n))
        landed = [ctx.enter_context(nc.semaphore(f"landed{s}")) for s in range(RING)]

        ring = sb("ring", RING * SLOT)
        cst = sb("cst", NCONST)
        bc = sb("bc", NBC)
        arena = sb("arena", 22 * 1024)
        vecT = sb("vecT", NVEC)
        rope = sb("rope", 128)
        stat = sb("stat", 128)
        slot_of = sb("slot_of", 2 * (E + 1))
        gate_of = sb("gate_of", 2 * (E + 1))
        flag_i = sb("flag_i", 100, I32, 1)
        pos_i = sb("pos_i", 2, I32)
        top_i = sb("top_i", 16, U32)
        top_v = sb("top_v", 16)
        PS = ctx.enter_context(nc.psum_tensor("PS", [P, 8, 512], F32))
        arena_byte, ring_byte = nc.lookup_mloc(arena).addr, nc.lookup_mloc(ring).addr

        def cc(at, n=P, parts=P):
            return cst[0:parts, at:at + n]

        ident = cc(C_ID)

        def area(at, n, parts=P):
            return arena[0:parts, at:at + n]

        def t3(ap, b):
            return ap.rearrange("p (b n) -> p b n", b=b)

        def banks(b, n):
            return PS[:, b:b + n, :].rearrange("p b n -> p (b n)")

        def parts_at(name, byte, cols):
            return nc.alloc_sbuf_tensor_at(name, [P, cols], F32R, offset=byte)[:, :]

        def pair(name, at_high, at_low, cols):
            return (parts_at(name + "_h", arena_byte + 4 * at_high, cols), parts_at(name + "_l", arena_byte + 4 * at_low, cols))

        X = area(0, 2048)
        XN = area(2048, 2048)
        XNT = pair("XNT", 4096, 6144, 2048)
        PR = [area(8192 + 1024 * g, 1024) for g in range(NSEG)]
        QKT = [area(15360 + 1024 * (s % 2), 1024) for s in range(4)]
        YT = pair("YT", 17408, 8192, 2048)
        SBT = [area(19456 + 768 * j, 768) for j in range(4)]
        WR = area(19456, 3072)
        YB = PR[3]
        VECS = area(19456, P, NVEC)
        TMP = area(2048, 1024)
        ROT = [area(3072 + 256 * j, 256) for j in range(4)]
        BUP = area(8192, 2048, E)
        BDN = area(10240, 1024, E)
        XG = area(11264, 512)
        SPT = area(11776, 256)
        GLU, SIG, LIN, HH = (area(12032 + 512 * j, 512) for j in range(4))
        HTS = area(14080, 512)
        YS = area(14592, 512)
        OH = area(15104, 256)
        OHG = area(15360, 256)
        SEL = area(15616, 64, E)
        GTT = area(15744, 256, E)
        EXM = area(16000, 64)
        MASK = area(16064, 64)
        logit = area(16128, 64)
        LGT = area(19456, 256, E)
        flag_f = area(16192, 100, 1)
        PIN = area(16384, 512)
        PT = pair("PT", 16896, 17408, 512)
        SG = area(8192, 2048)
        UB = area(8192, CC * 260).rearrange("p (c n) -> p c n", c=CC)
        XBT = area(11312, CC * 256).rearrange("p (c n) -> p c n", c=CC)
        QK = area(14384, 1280)
        VV = area(15664, 256)
        KD = area(15920, 512)
        ROT2 = [area(16432 + 160 * j, 160) for j in range(4)]
        QT = area(16432, 1024)
        KT = area(17456, 512)
        DT, ADT, CUM, CUMX, DTA = (area(17968 + 64 * j, 64) for j in range(5))
        AEX = area(17968 + 64 * 5, 32)
        PE_ = area(2048, 1024)
        PTS = area(3072, 1024)
        ATT = area(14384, 1024)
        ATTT = pair("ATTT", 2048, 3072, 1024)
        GATES = area(18432, 4096)
        DTT = area(18432, 256, 2 * SSDH)
        SQ2 = area(2048, 1280)
        Z = area(14384, 2048)
        CBM = area(16432, 1536)
        XS = area(11312, 2048)
        EE = [area(at, 768) for at in (8192, 8960, 13360)]
        WW = [area(9728 + 768 * j, 768) for j in range(2)]
        Y = area(4096, 2048)
        NY = area(8192, 2048)
        N1P = area(14384, 1024)
        ACTT = pair("ACTT", 8192, 8192 + FC * 256, FC * 256)
        SF = [area(19456 + 512 * j, 512) for j in range(2)]
        PROD = [area(20480 + 512 * j, 512) for j in range(2)]
        N2P = area(21504, 1024)

        HIGH = [parts_at(f"w_high{i}", ring_byte + 4 * SLOT * (RAW + i), SLOT) for i in range(BUF)]
        LOW = [parts_at(f"w_low{i}", ring_byte + 4 * SLOT * (RAW + BUF + i), SLOT) for i in range(BUF)]

        def slot(s):
            return ring[:, s * SLOT:(s + 1) * SLOT]

        def size(key):
            _, chunks, width = pieces[number[key]]
            return chunks * width

        def split_view(key):
            _, chunks, width = pieces[number[key]]
            return [x[number[key] % BUF][:, 0:chunks * width].rearrange("p (k n) -> p k n", k=chunks) for x in (HIGH, LOW)]

        def chain(eng, name):
            n = [0]

            def link(ins):
                n[0] += 1
                ins.then_inc(sem(name), 1)
                eng.wait_ge(sem(name), n[0])
            return link, n

        def bcast(ap, mid):
            return ap.unsqueeze(1).to_broadcast([ap.shape[0], mid, ap.shape[1]])

        def spread_last(ap, n):
            return ap.unsqueeze(2).to_broadcast([ap.shape[0], ap.shape[1], n])

        XBC_BANK = (2, 3, 4, 5, 0, 1)
        FILL = (1, 4, 7, 10)
        NORM_BANK = (4, 4, 4, 4, 0, 4)

        GAINS = [(B_SBQ, "sb_q_gain"), (B_SBK, "sb_k_gain"), (B_RQ, "ret_q_gain"), (B_RK, "ret_k_gain"),
                 (B_Q2, "q_norm_2"), (B_K2, "k_norm_2"), (B_GG, "ret_gn_gain"), (B_GB, "ret_gn_bias"),
                 (B_RT, "b_router"), (B_DTB, "dt_bias_f_2"), (B_DTB + SSDH, "dt_bias_b_2"),
                 (B_ALOG, "a_log_f_2"), (B_ALOG + SSDH, "a_log_b_2"), (B_DSK, "d_skip_2")]

        block = ctx.enter_context(nc.Block())

        @block.sync
        def _(sp):
            def load(key):
                src, chunks, width = pieces[number[key]]
                n, s = number[key], raw_slot(key)
                if late <= n < late + RAW:
                    j = EXPERT_SLOT.index(s)
                    sp.wait_ge(sem("w_used"), before_experts + PER_EXPERT * (ROUNDS - 1) + j + 1)
                elif n >= RAW:
                    sp.wait_ge(sem("w_low"), n - RAW + 1)
                sp.dma_start(slot(s)[:, 0:chunks * width].rearrange("p (k n) -> p k n", k=chunks), src).then_inc(landed[s], 16)

            sp.dma_start(t3(X, 2), a["x"][0].rearrange("(b p) d -> p b d", p=P)).then_inc(sem("x_in"), 16)
            sp.dma_start(cst[:, 0:C_EARLY], a["consts"][:, 0:C_EARLY]).then_inc(sem("consts"), 16)
            for key in keys[:3]:
                load(key)
            sp.dma_start(pos_i[:, :], a["positions"].rearrange("o (b p) -> p (o b)", p=P),
                         allow_slow_non_contiguous=True).then_inc(sem("gains"), 16)
            for at, name in GAINS:
                n = a[name].shape[1]
                sp.dma_start(bc[:, at:at + n], a[name].to_broadcast([P, n])).then_inc(sem("gains"), 16)
            for key in keys[3:RAW]:
                load(key)
            sp.dma_start(cst[:, C_EARLY:], a["consts"][:, C_EARLY:]).then_inc(sem("consts_late"), 16)
            for key in keys[RAW:late]:
                load(key)

            def expert_load(e, j):
                dst = slot(EXPERT_SLOT[j])
                if j < KC:
                    src = w_up[e, j * P:(j + 1) * P, :]
                else:
                    dst = dst.rearrange("p (k n) -> p k n", k=2)
                    src = w_down_e[e, (j - KC) * 256:(j - KC + 1) * 256, :].rearrange("(k p) n -> p k n", p=P)
                sp.dma_start(dst, src).then_inc(landed[EXPERT_SLOT[j]], 16)

            def expert_loads(e, turn):
                for j in range(PER_EXPERT):
                    sp.wait_ge(sem("w_used"), turn * PER_EXPERT + (before_experts - PER_EXPERT + j + 1))
                    expert_load(e, j)

            for j, s in enumerate(EXPERT_SLOT):
                if s < RAW:
                    sp.wait_ge(sem("w_low"), max(n for n in range(late) if n % RAW == s) + 1)
                else:
                    sp.wait_ge(sem("w_used"), before_experts)
                expert_load(0, j)
            with sp.Fori(1, n_experts) as e:
                expert_loads(e, e)
            sp.wait_ge(sem("flags"), 1)
            any_more = sp.value_load(flag_i[0:1, 96:97])
            with sp.If(any_more > 0):
                with sp.Fori(0, PASSES - 1) as p:
                    with sp.Fori(0, E) as e:
                        more = sp.value_load(flag_i[0:1, bass.ds(p * E + e, 1)])
                        with sp.If(more > 0):
                            expert_loads(e, p * E + e + E)
                            sp.wait_ge(sem("w_used"), (p * E + e) * PER_EXPERT + (before_experts + PER_EXPERT * (E + 1)))
                            sp.sem_inc(sem("pass_end"), 1)
                        with sp.Else():
                            sp.wait_ge(sem("w_used"), (p * E + e) * PER_EXPERT + (before_experts + PER_EXPERT * E))
                            for j in range(PER_EXPERT):
                                sp.sem_inc(landed[j], 16)
                        sp.nop()
                sp.nop()
            with sp.Else():
                sp.wait_ge(sem("w_used"), before_experts + PER_EXPERT * n_experts)
                for j in range(PER_EXPERT):
                    sp.sem_inc(landed[j], 16 * (PASSES - 1) * E)
            sp.nop()
            for key in keys[late:]:
                load(key)
            for tb in range(NTB):
                sp.wait_ge(sem("done"), tb + 1)
                sp.dma_start(out[0, tb * P:(tb + 1) * P, :], X[:, tb * D:(tb + 1) * D]).then_inc(sem("out_stored"), 16)
            sp.wait_ge(sem("out_stored"), 2 * 16)

        @block.tensor
        def _(pe):
            def arrived(key):
                pe.wait_ge(sem("w_low"), number[key] + 1)

            def product(out, lhs, rhs, start, stop):
                nc.tensor.matmul(out, lhs[0], rhs[0], start=start, stop=False)
                nc.tensor.matmul(out, lhs[0], rhs[1], start=False, stop=False)
                return nc.tensor.matmul(out, lhs[1], rhs[0], start=False, stop=stop)

            def transposes(src, bank, sem_name, ready, base):
                for tb in range(NTB):
                    pe.wait_ge(sem(ready), base + tb + 1)
                    for c in range(KC):
                        ins = nc.tensor.transpose(PS[:, bank + c // 2, (c % 2) * 256 + tb * P:(c % 2) * 256 + (tb + 1) * P],
                                                  t3(src, 2)[:, tb, c * P:(c + 1) * P], ident)
                        if tb == 1 and c % 2:
                            ins.then_inc(sem(sem_name), 1)

            def half_transposes(src, bank, sem_name):
                for c in range(4):
                    for tb in range(NTB):
                        ins = nc.tensor.transpose(PS[:, bank + c // 2, (c % 2) * 256 + tb * P:(c % 2) * 256 + (tb + 1) * P],
                                                  t3(src, 2)[:, tb, c * P:(c + 1) * P], ident)
                ins.then_inc(sem(sem_name), 1)

            def norm_T(i):
                transposes(NY if i == 4 else XN, NORM_BANK[i], "xnT_ps", "xn", 2 * i)

            def need_xnT(i):
                pe.wait_ge(sem("xnT"), 4 * (i + 1))

            def half_group(tag, g, half, lhs, bank_of, first=0, last=7, first_rows=False):
                key = (tag, g, half) if half is not None else (tag, g)
                arrived(key)
                w = split_view(key)
                h = half or 0
                for tb in range(NTB):
                    for k in range(4):
                        c = h * 4 + k
                        ins = product(PS[:, bank_of(tb), :], [x[:, c * 256 + tb * P:c * 256 + (tb + 1) * P] for x in lhs],
                                      [x[:, k, :] for x in w], start=c == first, stop=c == last)
                    if tb == 0 and first_rows:
                        ins.then_inc(sem("first_rows"), 1)
                ins.then_inc(sem("w_used"), 1)

            def feature_rows(key, bank):
                arrived(key)
                w = split_view(key)
                for c in range(2):
                    for k in range(KC):
                        ins = product(PS[:, bank, c * 256:(c + 1) * 256], [x[:, k, c * P:(c + 1) * P] for x in w],
                                      [x[:, k * 256:(k + 1) * 256] for x in XNT], start=k == 0, stop=k == KC - 1)
                ins.then_inc(sem("w_used"), 1)

            def narrow_rows(key, bank):
                arrived(key)
                w = split_view(key)
                for k in range(KC):
                    ins = product(PS[0:E, bank, 0:256], [x[:, k, :] for x in w],
                                  [x[:, k * 256:(k + 1) * 256] for x in XNT], start=k == 0, stop=k == KC - 1)
                ins.then_inc(sem("w_used"), 1)

            def narrow_transposes(src, bank, signal):
                for tb in range(NTB):
                    ins = nc.tensor.transpose(PS[:, bank, 256 + tb * E:256 + (tb + 1) * E], src[:, tb * P:(tb + 1) * P], cst[0:E, C_ID:C_ID + E])
                ins.then_inc(sem(signal), 1)

            def token_rows(key, bank, width):
                arrived(key)
                w = split_view(key)
                for tb in range(NTB):
                    for k in range(KC):
                        ins = product(PS[:, bank, tb * width:(tb + 1) * width],
                                      [x[:, k * 256 + tb * P:k * 256 + (tb + 1) * P] for x in XNT],
                                      [x[:, k, :] for x in w], start=k == 0, stop=k == KC - 1)
                ins.then_inc(sem("w_used"), 1)

            pe.wait_ge(sem("consts"), 16)
            pe.wait_ge(sem("vecs"), 128)
            nc.tensor.transpose(PS[:, 0, 0:NVEC], VECS, cst[0:NVEC, C_ID:C_ID + NVEC]).then_inc(sem("vecT_ps"), 1)
            norm_T(0)
            need_xnT(0)
            def seg(g, half):
                at = SEG_ORDER.index(g)
                if half == 0 and at >= 2:
                    pe.wait_ge(sem("proj_sb"), at - 1)
                half_group("in", g, half, XNT, lambda tb: 2 * (at % 2) + tb)

            def sb_z(b):
                if b == 0:
                    pe.wait_ge(sem("qkT"), 2)
                else:
                    pe.wait_ge(sem("sb_z_read"), b)
                for hh in range(2):
                    q = t3(QKT[0], 4)[64 * hh:64 * hh + 64, b, :]
                    k = t3(QKT[1], 4)[64 * hh:64 * hh + 64, b, :]
                    nc.tensor.matmul(PS[:, 4 + hh, 0:256], k[:, 0:P], q, start=True, stop=True)
                    ins = nc.tensor.matmul(PS[:, 4 + hh, 256:384], k[:, P:256], q[:, P:256], start=True, stop=True)
                ins.then_inc(sem("sb_z"), 1)

            def sb_tail(b):
                pe.wait_ge(sem("sb_m"), b + 1)
                if b:
                    pe.wait_ge(sem("yt"), b)
                m = t3(SBT[2], 2)
                for hh in range(2):
                    nc.tensor.matmul(PS[:, 6 + hh, 0:256], cc(C_GT), m[:, hh, 0:256], start=True, stop=False)
                    nc.tensor.matmul(PS[:, 6 + hh, P:256], cc(C_ONE), m[:, hh, 256:384], start=False, stop=True)
                    ins = nc.tensor.matmul(PS[:, 6 + hh, 256:384], cc(C_GT), m[:, hh, 256:384], start=True, stop=True)
                ins.then_inc(sem("sb_tail"), 1)

            def sb_pv(b):
                pe.wait_ge(sem("sb_w"), b + 1)
                w, v = t3(SBT[3], 2), t3(PR[2], 2)
                for hh in range(2):
                    c0 = (2 * b + hh) * HD
                    nc.tensor.matmul(PS[64 * hh:64 * hh + 64, 6, 0:256], v[:, 0, c0:c0 + HD], w[:, hh, 0:256], start=True, stop=False)
                    ins = nc.tensor.matmul(PS[64 * hh:64 * hh + 64, 6, P:256], v[:, 1, c0:c0 + HD], w[:, hh, 256:384], start=False, stop=True)
                ins.then_inc(sem("sb_pv"), 1)

            for g in SEG_ORDER[:3]:
                seg(g, 0), seg(g, 1)
            pe.wait_ge(sem("ret_qk"), 1)
            half_transposes(PR[0], 4, "qkT_ps")
            pe.wait_ge(sem("ret_qk"), 2)
            half_transposes(PR[1], 6, "qkT_ps")
            seg(2, 0)
            sb_z(0)
            seg(2, 1)
            pe.wait_ge(sem("consts_late"), 16)
            for b in range(3):
                seg(4 + b, 0)
                sb_tail(b)
                sb_z(b + 1)
                seg(4 + b, 1)
                sb_pv(b)
            pe.wait_ge(sem("ret_qk"), 3)
            pe.wait_ge(sem("proj_sb"), NSEG - 1)
            half_transposes(PR[3], 2, "qkT_ps")
            sb_tail(3)
            pe.wait_ge(sem("ret_qk"), 4)
            pe.wait_ge(sem("proj_sb"), NSEG)
            half_transposes(PR[4], 0, "qkT_ps")
            pe.wait_ge(sem("qkT"), 4)

            def ret_scores(h):
                if h >= 4:
                    pe.wait_ge(sem("ret_w"), h - 3)
                q = t3(QKT[2], 4)[64 * (h % 2):64 * (h % 2) + 64, h // 2, :]
                k = t3(QKT[3], 4)[64 * (h % 2):64 * (h % 2) + 64, h // 2, :]
                nc.tensor.matmul(PS[:, h % 4, 0:256], k[:, 0:P], q, start=True, stop=True)
                nc.tensor.matmul(PS[:, h % 4, 256:384], k[:, P:256], q[:, P:256], start=True, stop=True).then_inc(sem("ret_s"), 1)

            for h in range(4):
                ret_scores(h)
            sb_pv(3)
            v3 = t3(PR[5], 2)
            for h in range(NH):
                pe.wait_ge(sem("ret_w"), h + 1)
                w = WR[:, h * 384:(h + 1) * 384]
                c0, c1 = h * HD, (h + 1) * HD
                nc.tensor.matmul(PS[:, 4, c0:c1], w[:, 0:P], v3[:, 0, c0:c1], start=True, stop=True)
                nc.tensor.matmul(PS[:, 5, c0:c1], w[:, P:256], v3[:, 0, c0:c1], start=True, stop=False)
                ins = nc.tensor.matmul(PS[:, 5, c0:c1], w[:, 256:384], v3[:, 1, c0:c1], start=False, stop=True)
                if h + 4 < NH:
                    ret_scores(h + 4)
            ins.then_inc(sem("ret_y"), 1)
            pe.wait_ge(sem("yt"), 4)
            for g in range(2):
                half_group("out", g, 0, YT, lambda tb: 2 * tb + g)
            pe.wait_ge(sem("yb"), 1)
            half_transposes(YB, 6, "ybT_ps")
            pe.wait_ge(sem("ybT"), 1)
            for g in range(2):
                half_group("out", g, 1, YT, lambda tb: 2 * tb + g, first_rows=g == 1)
            norm_T(1)
            need_xnT(1)
            narrow_rows("router", 0)
            pe.wait_ge(sem("logitT"), 1)
            narrow_transposes(LGT, 0, "logit_ps")
            pe.wait_ge(sem("mask"), 1)
            m = t3(MASK, 2)
            nc.tensor.matmul(PS[:, 1, 0:E], cc(C_LT), m[:, 0, :], start=True, stop=True)
            nc.tensor.matmul(PS[:, 1, E:2 * E], cc(C_ONE), m[:, 0, :], start=True, stop=False)
            nc.tensor.matmul(PS[:, 1, E:2 * E], cc(C_LT), m[:, 1, :], start=False, stop=True)
            nc.tensor.matmul(PS[:, 1, 2 * E:3 * E], cc(C_ONE), m[:, 0, :], start=True, stop=False)
            nc.tensor.matmul(PS[:, 1, 2 * E:3 * E], cc(C_ONE), m[:, 1, :], start=False, stop=True).then_inc(sem("pos_ps"), 1)
            pe.wait_ge(sem("gates"), 1)
            for tb in range(NTB):
                ins = nc.tensor.transpose(PS[0:E, 2, tb * P:(tb + 1) * P], t3(gate_of[:, :], 2)[:, tb, 0:E], ident)
            ins.then_inc(sem("gT_ps"), 1)
            pe.wait_ge(sem("gT"), 1)
            pe.wait_ge(sem("flags"), 1)
            pe.wait_ge(sem("late_in"), 48)
            for tb in range(NTB):
                for n in range(2):
                    nc.tensor.matmul(PS[:, 2 * tb + n, :], GTT[:, tb * P:(tb + 1) * P], BDN[:, n * 512:(n + 1) * 512],
                                     start=True, stop=False, skip_group_check=True)

            def gather(sig):
                for c in range(KC):
                    for tb in range(NTB):
                        ins = nc.tensor.matmul(PS[:, 6, c * CAP:(c + 1) * CAP], t3(XN, 2)[:, tb, c * P:(c + 1) * P],
                                               OH[:, tb * P:tb * P + CAP], start=tb == 0, stop=tb == 1)
                ins.then_inc(sem(sig), 1)

            def spread(sig):
                for tb in range(NTB):
                    ins = nc.tensor.transpose(PS[:, 7, tb * P:(tb + 1) * P], OHG[:, tb * P:(tb + 1) * P], ident)
                ins.then_inc(sem(sig), 1)

            def up(turn):
                for n in range(4):
                    nc.tensor.matmul(PS[64 * (n % 2):64 * (n % 2) + 64, 4 + n // 2, :], SEL, BUP[:, n * 512:(n + 1) * 512],
                                     start=True, stop=False)
                for c in range(KC):
                    s = EXPERT_SLOT[c]
                    pe.wait_ge(landed[s], turn * 16 + 16 * (slot_fills(s) + 1))
                    w = slot(s)
                    for n in range(4):
                        ins = nc.tensor.matmul(PS[64 * (n % 2):64 * (n % 2) + 64, 4 + n // 2, :], XG[:, c * CAP:(c + 1) * CAP],
                                               w[:, n * 512:(n + 1) * 512], start=False, stop=c == KC - 1)
                    ins.then_inc(sem("w_used"), 1)

            def h_transposes(sig):
                for j in range(4):
                    ins = nc.tensor.transpose(PS[:, 6, j * P:(j + 1) * P], HH[:, j * P:(j + 1) * P], ident)
                ins.then_inc(sem(sig), 1)

            def down(turn):
                for j in range(4):
                    s = EXPERT_SLOT[KC + j]
                    pe.wait_ge(landed[s], turn * 16 + 16 * (slot_fills(s) + 1))
                    w = slot(s).rearrange("p (k n) -> p k n", k=2)
                    for k in range(2):
                        c = 2 * j + k
                        lhs = HTS[:, (c % 4) * P + CAP * (c // 4):(c % 4) * P + CAP * (c // 4) + CAP]
                        for n in range(2):
                            ins = nc.tensor.matmul(PS[64 * n:64 * n + 64, 7, :], lhs, w[:, k, n * 512:(n + 1) * 512],
                                                   start=c == 0, stop=c == KC - 1)
                    ins.then_inc(sem("w_used"), 1)

            def scatter(sig):
                for tb in range(NTB):
                    for n in range(2):
                        ins = nc.tensor.matmul(PS[:, 2 * tb + n, :], SPT[64 * n:64 * n + 64, tb * P:(tb + 1) * P],
                                               YS[64 * n:64 * n + 64, :], start=False, stop=False, skip_group_check=True)
                ins.then_inc(sem(sig), 1)

            pe.wait_ge(sem("onehot"), 1)
            gather("gathered")
            with pe.Fori(0, n_experts) as e:
                pe.wait_ge(sem("x_slots"), e + 1)
                pe.wait_ge(sem("sel"), e + 1)
                up(e)
                pe.wait_ge(sem("weighted"), e + 1)
                spread("spread")
                pe.wait_ge(sem("onehot"), e + 2)
                gather("gathered")
                pe.wait_ge(sem("h_done"), e + 1)
                pe.wait_ge(sem("x_slots"), e + 2)
                h_transposes("hT_ps")
                pe.wait_ge(sem("sT_slots"), e + 1)
                pe.wait_ge(sem("hT"), e + 1)
                down(e)
                pe.wait_ge(sem("y_slots"), e + 1)
                scatter("scattered")
            any_more = pe.value_load(flag_i[0:1, 96:97])
            with pe.If(any_more > 0):
                with pe.Fori(0, PASSES - 1) as p:
                    with pe.Fori(0, E) as e:
                        more = pe.value_load(flag_i[0:1, bass.ds(p * E + e, 1)])
                        with pe.If(more > 0):
                            t = p * E + e
                            pe.wait_ge(sem("ov_onehot"), t + 1)
                            gather("ov_gathered")
                            spread("ov_gathered")
                            pe.wait_ge(sem("ov_x"), t + 1)
                            up(t + E)
                            pe.wait_ge(sem("ov_h"), t + 1)
                            h_transposes("ov_hT_ps")
                            pe.wait_ge(sem("ov_hT"), t + 1)
                            down(t + E)
                            pe.wait_ge(sem("ov_y"), t + 1)
                            scatter("scattered")
                            pe.wait_ge(sem("scattered"), t + (n_experts + 1))
                            pe.sem_inc(sem("pass_end"), 1)
                        with pe.Else():
                            pe.sem_inc(sem("w_used"), PER_EXPERT)
                            pe.sem_inc(sem("ov_gathered"), 2)
                            pe.sem_inc(sem("ov_hT_ps"), 1)
                            pe.sem_inc(sem("scattered"), 1)
                        pe.nop()
                pe.nop()
            with pe.Else():
                pe.wait_ge(sem("scattered"), n_experts)
                pe.sem_inc(sem("w_used"), PER_EXPERT * (PASSES - 1) * E)
                pe.sem_inc(sem("scattered"), (PASSES - 1) * E)
            pe.nop()

            norm_T(2)
            need_xnT(2)
            for g in range(2):
                for half in range(2):
                    half_group("ple_gate", g, half, XNT, lambda tb: 2 * tb + g)
                if g == 0:
                    for kc in range(2):
                        for tb in range(NTB):
                            ins = nc.tensor.transpose(PS[:, 6, kc * 256 + tb * P:kc * 256 + (tb + 1) * P],
                                                      t3(PIN, 2)[:, tb, kc * P:(kc + 1) * P], ident)
                    ins.then_inc(sem("pT_ps"), 1)
            pe.wait_ge(sem("pT"), 1)
            arrived("ple_proj")
            w = split_view("ple_proj")
            for tb in range(NTB):
                for n in range(2):
                    for k in range(2):
                        ins = product(PS[:, 4 + 2 * tb + n, :], [x[:, k * 256 + tb * P:k * 256 + (tb + 1) * P] for x in PT],
                                      [x[:, k, n * 512:(n + 1) * 512] for x in w], start=k == 0, stop=k == 1)
                if tb == 0:
                    ins.then_inc(sem("first_rows"), 1)
            ins.then_inc(sem("w_used"), 1)

            norm_T(3)
            need_xnT(3)

            for half in range(2):
                half_group("q", 0, half, XNT, lambda tb: tb)
            token_rows("kv", 7, 256)
            narrow_rows("dt", 6)
            for c in range(6):
                if c == 4:
                    pe.wait_ge(sem("q_sb"), 1)
                feature_rows(("xbc", c), XBC_BANK[c])
                if c == 0:
                    pe.wait_ge(sem("dtT"), 1)
                    narrow_transposes(DTT, 6, "dt_ps")

            def gates(i):
                g, half = divmod(i, 2)
                if half == 0:
                    if g == 0:
                        pe.wait_ge(sem("kv_sb"), 1)
                        pe.wait_ge(sem("qk2T"), 1)
                    else:
                        pe.wait_ge(sem("gate2"), g)
                half_group("gates", g, half, XNT, lambda tb: 6 + tb)

            pe.wait_ge(sem("dt_abs"), 1)
            pe.wait_ge(sem("kv_sb"), 1)
            pe.wait_ge(sem("qk2"), 2)
            for c in range(4):
                for tb in range(NTB):
                    ins = nc.tensor.transpose(PS[:, 6 + c // 2, (c % 2) * 256 + tb * P:(c % 2) * 256 + (tb + 1) * P],
                                              t3(QK, 2)[:, tb, c * P:(c + 1) * P], ident)
            ins.then_inc(sem("qk2T_ps"), 1)
            pe.wait_ge(sem("xbc_sb"), 6)
            for kv in range(2):
                for tb in range(NTB):
                    ins = nc.tensor.transpose(PS[:, 2, kv * 256 + tb * P:kv * 256 + (tb + 1) * P],
                                              t3(KD, 2)[:, tb, kv * P:(kv + 1) * P], ident)
            ins.then_inc(sem("qk2T_ps"), 1)
            pe.wait_ge(sem("qk2T"), 2)
            adt = t3(ADT, 2)
            for u in range(4):
                tb, h0 = u // 2, 4 * (u % 2)
                if u >= 1:
                    pe.wait_ge(sem("p_exp"), 4 * u)
                for i in range(4):
                    h = h0 + i
                    r = 64 * (h % 2)
                    ins = nc.tensor.matmul(PS[:, i % 2, (i // 2) * 256:(i // 2) * 256 + 256],
                                           t3(QT, 4)[r:r + 64, h // 2, tb * P:(tb + 1) * P],
                                           t3(KT, 2)[r:r + 64, h // 4, :], start=True, stop=True)
                ins.then_inc(sem("s_ps"), 1)
                gates(2 * u)
                pe.wait_ge(sem("p_exp"), 4 * (u + 1))
                if u >= 1:
                    pe.wait_ge(sem("pT2"), u)
                for i in range(4):
                    for kb in range(2):
                        ins = nc.tensor.transpose(PS[:, 2 + i // 2, (i % 2) * 256 + kb * P:(i % 2) * 256 + (kb + 1) * P],
                                                  t3(PE_, 4)[:, i, kb * P:(kb + 1) * P], ident)
                ins.then_inc(sem("pT2_ps"), 1)
                gates(2 * u + 1)
                pe.wait_ge(sem("pT2"), u + 1)
                if u == 2:
                    pe.wait_ge(sem("cum_done"), 1)
                for i in range(4):
                    h = h0 + i
                    for kb in range(2):
                        ins = nc.tensor.matmul(PS[:, 4 + tb, h * HD:(h + 1) * HD], t3(PTS, 4)[:, i, kb * P:(kb + 1) * P],
                                               t3(VV, 2)[:, kb, (h // 4) * HD:(h // 4 + 1) * HD], start=kb == 0, stop=kb == 1)
                ins.then_inc(sem("o_ps"), 1)
                if u == 0:
                    pe.wait_ge(sem("adt"), 1)
                    for tb in range(NTB):
                        nc.tensor.matmul(PS[:, 5, tb * 32:tb * 32 + 16], cc(C_LE), adt[:, tb, 0:16], start=True, stop=True)
                        nc.tensor.matmul(PS[:, 5, tb * 32 + 16:tb * 32 + 32], cc(C_GE), adt[:, tb, 16:32], start=True, stop=True)
                        ins = nc.tensor.matmul(PS[:, 5, 64 + tb * 32:96 + tb * 32], cc(C_ONE), adt[:, tb, :], start=True, stop=True)
                    ins.then_inc(sem("cum_ps"), 1)

            pe.wait_ge(sem("silu_c"), CC)
            pe.wait_ge(sem("pT2"), 4)
            for c in range(KC):
                for tb in range(NTB):
                    ins = nc.tensor.transpose(PS[:, 2 * tb + c // 4, (c % 4) * P:(c % 4 + 1) * P],
                                              XBT[:, c, tb * P:(tb + 1) * P], ident)
            ins.then_inc(sem("xs_ps"), 1)
            pe.wait_ge(sem("gate2"), 4)
            for g in range(2):
                for s in range(2):
                    ins = nc.tensor.matmul(PS[:, 6 + g, s * 256:(s + 1) * 256], XBT[:, 8 + g, s * P:(s + 1) * P],
                                           XBT[:, 10 + g, :], start=True, stop=True)
            ins.then_inc(sem("cb_ps"), 1)
            pe.wait_ge(sem("att"), 1)
            half_transposes(ATT, 4, "attT_ps")
            pe.wait_ge(sem("attT"), 1)

            def abc(h):
                if h >= 2:
                    pe.wait_ge(sem("e_sub"), h - 1)
                for d in range(2):
                    for tb in range(NTB):
                        ins = nc.tensor.matmul(PS[:, 4 + h % 2, d * 256 + tb * P:d * 256 + (tb + 1) * P],
                                               adt[:, tb, d * 16 + h:d * 16 + h + 1].to_broadcast([P, P]),
                                               cc(C_LE if d == 0 else C_GE), start=True, stop=True)
                ins.then_inc(sem("abc"), 1)

            abc(0), abc(1)
            pe.wait_ge(sem("xs"), 1)
            pe.wait_ge(sem("cb"), 1)
            abc(2)
            xs = t3(XS, 2)
            for h in range(SSDH):
                if h + 3 < SSDH:
                    abc(h + 3)
                if h in FILL:
                    g, half = divmod(FILL.index(h), 2)
                    if (g, half) == (1, 0):
                        pe.wait_ge(sem("z_sb"), 1)
                    half_group("z", g, half, XNT, lambda tb: 6 + tb)
                pe.wait_ge(sem("w_ssd"), h + 1)
                w = WW[h % 2]
                n, c0 = h // 8, (h % 8) * HD
                for tb, terms in ((0, ((0, 0), (3, 0), (5, 1))), (1, ((1, 0), (2, 1), (4, 1)))):
                    for i, (blk, s) in enumerate(terms):
                        ins = nc.tensor.matmul(PS[:, 2 * tb + n, c0:c0 + HD], w[:, blk * P:(blk + 1) * P],
                                               xs[:, s, h * HD:(h + 1) * HD], start=i == 0, stop=i == 2)
                ins.then_inc(sem("y_ssd"), 1)
            half_group("attn_proj", 0, None, ATTT, lambda tb: 4 + tb, last=3)
            pe.wait_ge(sem("z_sb"), 2)
            half_group("attn_proj", 1, None, ATTT, lambda tb: 6 + tb, last=3)
            norm_T(4)
            need_xnT(4)
            pe.wait_ge(sem("attn_out"), 2)
            for g in range(2):
                for half in range(2):
                    half_group("ssd_proj", g, half, XNT, lambda tb: 4 + 2 * tb + g, first_rows=(g, half) == (1, 1))
            transposes(XN, 0, "mixT_ps", "mixed", 0)
            pe.wait_ge(sem("mixT"), 4)
            for g in range(2):
                for half in range(2):
                    half_group("out2", g, half, XNT, lambda tb: 2 * tb + g, first_rows=(g, half) == (1, 1))
            norm_T(5)
            need_xnT(5)
            for j in range(FC // 2):
                if j >= 4:
                    pe.wait_ge(sem("ffn_act"), j - 3)
                feature_rows(("gate", j), 2 * (j % 4))
                feature_rows(("up", j), 2 * (j % 4) + 1)
            pe.wait_ge(sem("ffn_act"), FC // 2 - 1)
            for j in range(FC // 2):
                if j == FC // 2 - 1:
                    pe.wait_ge(sem("ffn_act"), FC // 2)
                arrived(("ffn_down", j))
                w = split_view(("ffn_down", j))
                for k in range(2):
                    f = 2 * j + k
                    for tb in range(NTB):
                        for n in range(2):
                            ins = product(PS[:, 2 * tb + n, :], [x[:, f * 256 + tb * P:f * 256 + (tb + 1) * P] for x in ACTT],
                                          [x[:, k, n * 512:(n + 1) * 512] for x in w], start=f == 0, stop=f == FC - 1)
                ins.then_inc(sem("w_used"), 1)

        @block.scalar
        def _(act):
            link, _n = chain(act, "act_step")
            eps = cc(C_EPS, 1)

            vec_rows = [(V_MIX, KC, a["g_mix_norm"][0].rearrange("(r n) -> r n", n=P)),
                        (V_FFN, KC, a["g_ffn_norm"][0].rearrange("(r n) -> r n", n=P)),
                        (V_PLE, KC, a["g_ple_norm"][0].rearrange("(r n) -> r n", n=P)),
                        (V_SSD, KC, a["ssd_norm_2"][0].rearrange("(r n) -> r n", n=P)),
                        (V_N1, KC, a["norm1_pre_2"][0].rearrange("(r n) -> r n", n=P)),
                        (V_N2, KC, a["norm2_pre_2"][0].rearrange("(r n) -> r n", n=P)),
                        (V_CW, CONVK * CC, a["conv_w_2"][0].rearrange("k (r n) -> (k r) n", n=P)),
                        (V_CB, CC, a["conv_b_2"][0].rearrange("(r n) -> r n", n=P))]
            for at, rows, src in vec_rows:
                act.dma_start(VECS[at:at + rows, :], src).then_inc(sem("vecs"), 16)
            done_splits = [0]

            def split_to(n):
                while done_splits[0] <= min(n, len(keys) - 1):
                    m = done_splits[0]
                    key = keys[m]
                    if late <= m < late + BUF:
                        act.wait_ge(sem("w_used"), before_experts + PER_EXPERT * ROUNDS)
                    elif m >= BUF:
                        act.wait_ge(sem("w_used"), place[keys[m - BUF]] + 1)
                    act.wait_ge(landed[raw_slot(key)], landed_by(key))
                    nc.scalar.activation(HIGH[m % BUF][:, 0:size(key)], slot(raw_slot(key))[:, 0:size(key)], ACT.Copy).then_inc(sem("w_high"), 1)
                    done_splits[0] += 1

            def load_table(func):
                link(nc.scalar.activation(stat[:, 122:123], eps, func))

            def norm(i, ready, src=X, scratch=XN):
                load_table(ACT.Sqrt)
                for tb in range(NTB):
                    if ready:
                        act.wait_ge(sem(ready), tb + 1)
                    link(nc.scalar.activation(scratch[:, tb * D:(tb + 1) * D], src[:, tb * D:(tb + 1) * D], ACT.Square,
                                              accum_out=stat[:, tb:tb + 1]))
                    nc.scalar.activation(stat[:, 2 + tb:3 + tb], stat[:, tb:tb + 1], ACT.Sqrt, scale=1.0 / D,
                                         bias=eps).then_inc(sem("rms"), 1)

            def norm_evac(i, gain):
                for b in range(4):
                    act.wait_ge(sem("xnT_ps"), 4 * i + b + 1)
                    for c in (2 * b, 2 * b + 1):
                        ins = nc.scalar.activation(XNT[0][:, c * 256:(c + 1) * 256], PS[:, NORM_BANK[i] + b, (c % 2) * 256:(c % 2) * 256 + 256],
                                                   ACT.Copy, scale=vecT[:, gain + c:gain + c + 1])
                    ins.then_inc(sem("xnT_high"), 1)

            def head_sd(i, n):
                act.wait_ge(sem("head_sq"), i)
                nc.scalar.activation(stat[:, 32:32 + n], stat[:, 8:8 + n], ACT.Sqrt, scale=1.0 / HD, bias=eps).then_inc(sem("head_sd"), 1)

            def group_out(at):
                g = SEG_ORDER[at]
                split_to(2 * at + 4)
                act.wait_ge(sem("w_used"), place[("in", g, 1)] + 1)
                nc.scalar.activation(PR[g], banks(2 * (at % 2), 2), ACT.Silu if g == NSEG - 1 else ACT.Copy).then_inc(sem("proj_sb"), 1)

            act.wait_ge(sem("consts"), 16)
            load_table(ACT.Sqrt)
            act.wait_ge(sem("x_in"), 16)
            norm(0, None)
            split_to(2)
            act.wait_ge(sem("vecT"), 1)
            norm_evac(0, V_MIX)
            group_out(0)
            act.wait_ge(sem("trig_r"), 1)
            nc.scalar.activation(rope[:, 64:128], TMP[:, 0:64], ACT.Sin).then_inc(sem("trig"), 1)
            nc.scalar.activation(rope[:, 0:64], TMP[:, 0:64], ACT.Sin, scale=0.5).then_inc(sem("trig"), 1)
            head_sd(1, 16)
            group_out(1)
            head_sd(2, 16)
            group_out(2)
            head_sd(3, 16)
            split_to(9)
            z = PS[:, 4:6, 0:384]
            t0 = t3(SBT[0], 2)

            def sb_softplus(b):
                act.wait_ge(sem("sb_z"), b + 1)
                nc.scalar.activation(t0, z, ACT.Abs, scale=HD ** -0.5).then_inc(sem("sb_a"), 1)
                act.wait_ge(sem("sb_a"), b + 1)
                link(nc.scalar.activation(t0, t0, ACT.Exp, scale=-1.0))
                nc.scalar.activation(t0, t0, ACT.Ln, bias=1.0).then_inc(sem("sb_l"), 1)

            sb_softplus(0)
            for b in range(4):
                if b == 0:
                    group_out(3)
                if b < 3:
                    split_to(11 + 2 * b)
                act.wait_ge(sem("sb_t"), b + 1)
                nc.scalar.activation(SBT[3], SBT[3], ACT.Exp).then_inc(sem("sb_e"), 1)
                if b < 3:
                    sb_softplus(b + 1)
                    group_out(4 + b)
                act.wait_ge(sem("sb_pv"), b + 1)
                nc.scalar.activation(YT[0][:, b * 256:(b + 1) * 256], PS[:, 6, 0:256], ACT.Copy).then_inc(sem("yt_high"), 1)
                if b == 1:
                    head_sd(4, 16)
            head_sd(5, 16)
            split_to(before_experts - 1)
            act.wait_ge(sem("ybT_ps"), 1)
            nc.scalar.activation(YT[0][:, 1024:2048], banks(6, 2), ACT.Copy).then_inc(sem("ybT_high"), 1)

            norm(1, "x1")
            act.dma_start(BUP, a["b_up_gate"][0]).then_inc(sem("late_in"), 16)
            act.dma_start(BDN, a["b_down"][0]).then_inc(sem("late_in"), 16)
            act.dma_start(t3(PIN, 2), a["p"][0][0].rearrange("(b p) d -> p b d", p=P)).then_inc(sem("late_in"), 16)
            norm_evac(1, V_FFN)
            act.wait_ge(sem("w_used"), place["router"] + 1)
            nc.scalar.activation(LGT, PS[0:E, 0, 0:256], ACT.Copy).then_inc(sem("logitT"), 1)
            load_table(ACT.Exp)
            act.wait_ge(sem("neg_max"), 1)
            for tb in range(NTB):
                nc.scalar.activation(EXM[:, tb * E:(tb + 1) * E], logit[:, tb * E:(tb + 1) * E], ACT.Exp,
                                     bias=stat[:, 4 + tb:5 + tb]).then_inc(sem("ex"), 1)
            act.wait_ge(sem("gT_ps"), 1)
            nc.scalar.activation(GTT, PS[0:E, 2, 0:256], ACT.Copy).then_inc(sem("gT"), 1)

            def sigmoid(sig_in, sig_out, value):
                act.wait_ge(sem(sig_in), value)
                nc.scalar.activation(SIG, GLU, ACT.Sigmoid, scale=1.702).then_inc(sem(sig_out), 1)

            with act.Fori(0, n_experts) as e:
                sigmoid("glu", "sig", e + 1)
                act.wait_ge(sem("spread"), e + 1)
                nc.scalar.activation(SPT, PS[:, 7, 0:256], ACT.Copy).then_inc(sem("sT_slots"), 1)
                act.wait_ge(sem("hT_ps"), e + 1)
                nc.scalar.activation(HTS, PS[:, 6, :], ACT.Copy).then_inc(sem("hT"), 1)
            act.wait_ge(sem("flags"), 1)
            any_more = act.value_load(flag_i[0:1, 96:97])
            with act.If(any_more > 0):
                with act.Fori(0, PASSES - 1) as p:
                    with act.Fori(0, E) as e:
                        more = act.value_load(flag_i[0:1, bass.ds(p * E + e, 1)])
                        with act.If(more > 0):
                            t = p * E + e
                            act.wait_ge(sem("ov_gathered"), t * 2 + 2)
                            nc.scalar.activation(SPT, PS[:, 7, 0:256], ACT.Copy).then_inc(sem("sT_slots"), 1)
                            act.wait_ge(sem("sT_slots"), t + (n_experts + 1))
                            sigmoid("ov_glu", "ov_sig", t + 1)
                            act.wait_ge(sem("ov_hT_ps"), t + 1)
                            nc.scalar.activation(HTS, PS[:, 6, :], ACT.Copy).then_inc(sem("ov_hT"), 1)
                            act.wait_ge(sem("ov_hT"), t + 1)
                            act.sem_inc(sem("pass_end"), 1)
                        with act.Else():
                            act.sem_inc(sem("sT_slots"), 1)
                            act.sem_inc(sem("ov_sig"), 1)
                            act.sem_inc(sem("ov_hT"), 1)
                        act.nop()
                act.nop()
            with act.Else():
                act.nop()
            act.nop()

            split_to(late)
            norm(2, "x2")
            split_to(late + 1)
            norm_evac(2, V_PLE)
            split_to(number[("ple_proj")])
            act.wait_ge(sem("pT_ps"), 1)
            nc.scalar.activation(PT[0], PS[:, 6, :], ACT.Copy).then_inc(sem("pT_high"), 1)
            split_to(number[("ple_gate", 1, 1)] + 3)
            act.wait_ge(sem("w_used"), place[("ple_gate", 1, 1)] + 1)
            nc.scalar.activation(SG, banks(0, 4), ACT.Sigmoid).then_inc(sem("ple_gate"), 1)
            split_to(number["ple_proj"] + 3)
            norm(3, "x3")
            norm_evac(3, V_N1)
            split_to(number[("q", 0, 1)] + 3)
            act.wait_ge(sem("w_used"), place[("q", 0, 1)] + 1)
            nc.scalar.activation(t3(QK, 2)[:, :, 0:512], PS[:, 0:2, :], ACT.Copy).then_inc(sem("q_sb"), 1)
            split_to(number["kv"] + 3)
            act.wait_ge(sem("w_used"), place["kv"] + 1)
            kv = PS[:, 7, :].rearrange("p (b n) -> p b n", b=2)
            link(nc.scalar.activation(t3(QK, 2)[:, :, 512:640], kv[:, :, 0:P], ACT.Copy))
            nc.scalar.activation(t3(VV, 2), kv[:, :, P:256], ACT.Copy).then_inc(sem("kv_sb"), 1)
            head_sd(6, 20)
            split_to(number["dt"] + 3)
            act.wait_ge(sem("w_used"), place["dt"] + 1)
            nc.scalar.activation(DTT, PS[0:32, 6, 0:256], ACT.Copy).then_inc(sem("dtT"), 1)
            for c in range(6):
                split_to(number[("xbc", c)] + 3)
                act.wait_ge(sem("w_used"), place[("xbc", c)] + 1)
                nc.scalar.activation(UB[:, 2 * c:2 * c + 2, 2:258], PS[:, XBC_BANK[c], :].rearrange("p (c n) -> p c n", c=2),
                                     ACT.Copy).then_inc(sem("xbc_sb"), 1)
                if c == 0:
                    act.wait_ge(sem("dt_abs"), 1)
                    link(nc.scalar.activation(DTA, DT, ACT.Abs))
                    link(nc.scalar.activation(DTA, DTA, ACT.Exp, scale=-1.0))
                    nc.scalar.activation(DTA, DTA, ACT.Ln, bias=1.0).then_inc(sem("a_exp"), 1)
                    nc.scalar.activation(AEX, bc[:, B_ALOG:B_ALOG + 32], ACT.Exp).then_inc(sem("a_exp"), 1)

            silus = iter(range(CC))

            def conv_silu(n):
                for _ in range(n):
                    c = next(silus)
                    act.wait_ge(sem("conv"), c + 1)
                    nc.scalar.activation(XBT[:, c, :], XBT[:, c, :], ACT.Silu).then_inc(sem("silu_c"), 1)

            gates4 = GATES.rearrange("p (b n) -> p b n", b=2)
            for u in range(4):
                act.wait_ge(sem("s_max"), u + 1)
                for i in range(4):
                    at = 60 + 4 * u + 2 * (i % 2) + i // 2
                    nc.scalar.activation(t3(PE_, 4)[:, i, :], PS[:, i % 2, (i // 2) * 256:(i // 2) * 256 + 256], ACT.Exp,
                                         scale=HD ** -0.5, bias=stat[:, at:at + 1],
                                         accum_out=stat[:, 80 + 4 * u + i:81 + 4 * u + i]).then_inc(sem("p_exp"), 1)
                split_to(number[("gates", u, 0)] + 3)
                act.wait_ge(sem("pT2_ps"), u + 1)
                nc.scalar.activation(PTS, banks(2, 2), ACT.Copy).then_inc(sem("pT2"), 1)
                if u in (1, 2):
                    conv_silu(CC // 2)
                split_to(number[("gates", u, 1)] + 3)
                act.wait_ge(sem("w_used"), place[("gates", u, 1)] + 1)
                nc.scalar.activation(gates4[:, :, u * 512:(u + 1) * 512], PS[:, 6:8, :], ACT.Sigmoid).then_inc(sem("gate2"), 1)
            act.wait_ge(sem("xs_ps"), 1)
            nc.scalar.activation(XS, banks(0, 4), ACT.Copy).then_inc(sem("xs"), 1)
            act.wait_ge(sem("attT_ps"), 1)
            nc.scalar.activation(ATTT[0], banks(4, 2), ACT.Copy).then_inc(sem("attT_high"), 1)
            z4 = t3(Z, 2)
            for h in range(SSDH):
                act.wait_ge(sem("e_sub"), h + 1)
                nc.scalar.activation(EE[h % 3], EE[h % 3], ACT.Exp).then_inc(sem("e_exp"), 1)
                if h - 2 in FILL:
                    split_to(number[("z", 0, 0)] + FILL.index(h - 2) + 3)
                if h - 2 in (FILL[1], FILL[3]):
                    g = FILL.index(h - 2) // 2
                    act.wait_ge(sem("w_used"), place[("z", g, 1)] + 1)
                    nc.scalar.activation(z4[:, :, g * 512:(g + 1) * 512], PS[:, 6:8, :], ACT.Silu).then_inc(sem("z_sb"), 1)
            split_to(number[("attn_proj", 0)] + 3)
            norm(4, "y_mul", Y, NY)
            act.dma_start(N1P, a["norm1_post_2"].to_broadcast([P, D])).then_inc(sem("post1_in"), 16)
            split_to(number[("attn_proj", 1)] + 3)
            norm_evac(4, V_SSD)
            split_to(number[("ssd_proj", 1, 1)] + 2)
            for b in range(4):
                act.wait_ge(sem("mixT_ps"), b + 1)
                nc.scalar.activation(XNT[0][:, b * 512:(b + 1) * 512], PS[:, b, :], ACT.Copy).then_inc(sem("mixT_high"), 1)
            act.dma_start(N2P, a["norm2_post_2"].to_broadcast([P, D])).then_inc(sem("post2_in"), 16)

            def post_norm(key, first_rows):
                split_to(number[key] + 2)
                load_table(ACT.Sqrt)
                for tb in range(NTB):
                    if tb == 0 and first_rows:
                        act.wait_ge(sem("first_rows"), first_rows)
                    else:
                        act.wait_ge(sem("w_used"), place[key] + 1)
                    link(nc.scalar.activation(XN[:, tb * D:(tb + 1) * D], banks(2 * tb, 2), ACT.Square,
                                              accum_out=stat[:, tb:tb + 1]))
                    nc.scalar.activation(stat[:, 2 + tb:3 + tb], stat[:, tb:tb + 1], ACT.Sqrt, scale=1.0 / D,
                                         bias=eps).then_inc(sem("post_sd"), 1)

            post_norm(("out2", 1, 1), 4)
            norm(5, "x4")
            split_to(number[("out2", 1, 1)] + 3)
            norm_evac(5, V_N2)
            for j in range(FC // 2):
                split_to(number[("gate", j)] + 3)
                act.wait_ge(sem("w_used"), place[("gate", j)] + 1)
                if j >= 2:
                    act.wait_ge(sem("ffn_act"), j - 1)
                nc.scalar.activation(SF[j % 2], PS[:, 2 * (j % 4), :], ACT.Silu).then_inc(sem("silu_f"), 1)
                split_to(number[("up", j)] + 3)
            post_norm(("ffn_down", FC // 2 - 1), 0)

        @block.vector
        def _(dve):
            link, count = chain(dve, "dve_step")
            V = nc.vector
            tt, ts, stt = V.tensor_tensor, V.tensor_scalar, V.scalar_tensor_tensor

            def norm(i, src=X, dst=XN):
                for tb in range(NTB):
                    dve.wait_ge(sem("rms"), 2 * i + tb + 1)
                    link(V.reciprocal(stat[:, 6 + tb:7 + tb], stat[:, 2 + tb:3 + tb]))
                    ts(dst[:, tb * D:(tb + 1) * D], src[:, tb * D:(tb + 1) * D], stat[:, 6 + tb:7 + tb], None, ALU.mult).then_inc(sem("xn"), 1)

            def low(out, value, high):
                return tt(out, value, high.bitcast(F32), ALU.subtract)

            def norm_evac(i, gain):
                for b in range(4):
                    dve.wait_ge(sem("xnT_high"), 4 * i + b + 1)
                    for c in (2 * b, 2 * b + 1):
                        cols = slice(c * 256, (c + 1) * 256)
                        ins = stt(XNT[1][:, cols], PS[:, NORM_BANK[i] + b, (c % 2) * 256:(c % 2) * 256 + 256],
                                  vecT[:, gain + c:gain + c + 1], XNT[0][:, cols].bitcast(F32), ALU.mult, ALU.subtract)
                    ins.then_inc(sem("xnT"), 1)

            n_head = [0]

            def head_squares(src, n, tmp):
                link(tt(tmp, src, src, ALU.mult))
                n_head[0] += 1
                V.reduce_sum(stat[:, 8:8 + n], tmp.rearrange("p (h d) -> p h d", d=HD), AX.X).then_inc(sem("head_sq"), 1)

            def head_scale(src, n, gains):
                dve.wait_ge(sem("head_sd"), n_head[0])
                link(V.reciprocal(stat[:, 8:8 + n], stat[:, 32:32 + n]))
                s3 = src.rearrange("p (h d) -> p h d", d=HD)
                link(tt(s3, s3, spread_last(stat[:, 8:8 + n], HD), ALU.mult))
                for s, g in gains:
                    ins = tt(s, s, g, ALU.mult)
                return ins

            def rotate(x0, x1, cos, sin, tmp):
                t = tmp
                link(tt(t[0], x0, cos, ALU.mult))
                link(tt(t[1], x1, sin, ALU.mult))
                link(tt(t[2], x1, cos, ALU.mult))
                link(tt(t[3], x0, sin, ALU.mult))
                link(tt(x0, t[0], t[1], ALU.subtract))
                return tt(x1, t[2], t[3], ALU.add)

            dve.wait_ge(sem("consts"), 16)
            dve.wait_ge(sem("vecT_ps"), 1)
            V.tensor_copy(vecT[:, :], PS[:, 0, 0:NVEC]).then_inc(sem("vecT"), 1)
            dve.wait_ge(sem("vecT"), 1)
            norm(0)
            norm_evac(0, V_MIX)
            dve.wait_ge(sem("gains"), (1 + len(GAINS)) * 16)
            dve.wait_ge(sem("consts_late"), 16)
            link(V.tensor_copy(stat[:, 100:102], pos_i[:, :]))
            for tb in range(NTB):
                link(ts(TMP[:, tb * 32:(tb + 1) * 32], cc(C_FRQ, 32), stat[:, 100 + tb:101 + tb], None, ALU.mult))
            ang, turns = TMP[:, 0:64], TMP[:, 64:128]
            link(ts(turns, ang, TWO_PI_INV, ROUND, ALU.mult, ALU.add))
            link(ts(turns, turns, ROUND, None, ALU.subtract))
            for part in (PI2_A, PI2_B, PI2_C):
                link(stt(ang, turns, -part, ang, ALU.mult, ALU.add))
            ts(ang, ang, PI_IN, -PI_IN, ALU.min, ALU.max).then_inc(sem("trig_r"), 1)
            dve.wait_ge(sem("trig"), 2)
            cos, sin = rope[:, 0:64], rope[:, 64:128]
            link(tt(cos, cos, cos, ALU.mult))
            link(ts(cos, cos, -2.0, 1.0, ALU.mult, ALU.add))

            def gain3(at, n):
                return bcast(bc[:, at:at + HD], n)

            def heads(ap):
                return ap.rearrange("p (h d) -> p h d", d=HD)

            def qkT_evac(i, bank):
                dve.wait_ge(sem("qkT_ps"), i + 1)
                V.tensor_copy(QKT[i], banks(bank, 2)).then_inc(sem("qkT"), 1)

            def ret_rotate(s):
                for tb in range(NTB):
                    x = PR[s][:, tb * 512:(tb + 1) * 512].rearrange("p (h b d) -> p h b d", h=NH, b=2)
                    c3, s3 = (bcast(v[:, tb * 32:(tb + 1) * 32], NH) for v in (cos, sin))
                    ins = rotate(x[:, :, 0, :], x[:, :, 1, :], c3, s3, [r.rearrange("p (h d) -> p h d", h=NH) for r in ROT])
                    if tb == 0:
                        link(ins)
                ins.then_inc(sem("ret_qk"), 1)
                dve.wait_ge(sem("ret_qk"), s)

            for g, gain in ((0, B_SBQ), (1, B_SBK)):
                dve.wait_ge(sem("proj_sb"), g + 1)
                head_squares(PR[g], 16, TMP)
                head_scale(PR[g], 16, [(heads(PR[g]), gain3(gain, 16))]).then_inc(sem("ret_qk"), 1)
            qkT_evac(0, 4)
            qkT_evac(1, 6)
            dve.wait_ge(sem("proj_sb"), 3)
            head_squares(PR[3], 16, TMP)
            link(head_scale(PR[3], 16, [(heads(PR[3]), gain3(B_RQ, 16))]))
            ret_rotate(3)
            z, tail = PS[:, 4:6, 0:384], PS[:, 6:8, 0:384]
            t0, t1, t2, t3_ = (t3(x, 2) for x in SBT)
            sbm = bcast(cc(C_SBM, 384), 2)

            def yt_low(b):
                dve.wait_ge(sem("yt_high"), b + 1)
                cols = slice(b * 256, (b + 1) * 256)
                low(YT[1][:, cols], PS[:, 6, 0:256], YT[0][:, cols]).then_inc(sem("yt"), 1)

            for b in range(4):
                dve.wait_ge(sem("sb_a"), b + 1)
                link(ts(t1, z, HD ** -0.5, 0.0, ALU.mult, ALU.max))
                dve.wait_ge(sem("sb_l"), b + 1)
                link(tt(t1, t1, t0, ALU.add))
                tt(t2, t1, sbm, ALU.mult).then_inc(sem("sb_m"), 1)
                if b == 3:
                    qkT_evac(2, 2)
                if b:
                    yt_low(b - 1)
                dve.wait_ge(sem("dve_step"), count[0])
                stt(t3_, z, HD ** -0.5, t1, ALU.mult, ALU.subtract).then_inc(sem("sb_z_read"), 1)
                if b == 2:
                    link(head_scale(PR[4], 16, [(heads(PR[4]), gain3(B_RK, 16))]))
                dve.wait_ge(sem("sb_z_read"), b + 1)
                dve.wait_ge(sem("sb_tail"), b + 1)
                tt(t3_, t3_, tail, ALU.add).then_inc(sem("sb_t"), 1)
                if b == 3:
                    qkT_evac(3, 0)
                dve.wait_ge(sem("sb_e"), b + 1)
                stt(t3_, t3_, -1.0, sbm, ALU.mult, ALU.mult).then_inc(sem("sb_w"), 1)
                if b == 1:
                    dve.wait_ge(sem("proj_sb"), 5)
                    head_squares(PR[4], 16, TMP)
                if b == 2:
                    ret_rotate(4)
            for h in range(NH):
                if h == 4:
                    yt_low(3)
                dve.wait_ge(sem("ret_s"), h + 1)
                dm = cc(C_DM + h * 256, 256)
                w = WR[:, h * 384:(h + 1) * 384]
                tt(w[:, 0:256], PS[:, h % 4, 0:256], dm, ALU.mult)
                tt(w[:, 256:384], PS[:, h % 4, 256:384], dm[:, 0:P], ALU.mult).then_inc(sem("ret_w"), 1)
            dve.wait_ge(sem("ret_y"), 1)
            y = PS[:, 4:6, :].rearrange("p b (h d) -> p (b h) d", d=HD)
            yb3 = heads(YB)
            link(V.reduce_sum(stat[:, 8:24], y, AX.X))
            link(ts(stat[:, 8:24], stat[:, 8:24], 1.0 / HD, None, ALU.mult))
            link(tt(yb3, y, spread_last(stat[:, 8:24], HD), ALU.subtract))
            link(tt(TMP, YB, YB, ALU.mult))
            n_head[0] += 1
            V.reduce_sum(stat[:, 8:24], heads(TMP), AX.X).then_inc(sem("head_sq"), 1)
            dve.wait_ge(sem("head_sd"), n_head[0])
            link(V.reciprocal(stat[:, 8:24], stat[:, 32:48]))
            link(tt(yb3, yb3, spread_last(stat[:, 8:24], HD), ALU.mult))
            link(tt(t3(YB, 2), t3(YB, 2), bcast(bc[:, B_GG:B_GG + 512], 2), ALU.mult))
            link(tt(t3(YB, 2), t3(YB, 2), bcast(bc[:, B_GB:B_GB + 512], 2), ALU.add))
            dve.wait_ge(sem("proj_sb"), NSEG)
            tt(YB, YB, PR[6], ALU.mult).then_inc(sem("yb"), 1)
            dve.wait_ge(sem("ybT_high"), 1)
            low(YT[1][:, 1024:2048], banks(6, 2), YT[0][:, 1024:2048]).then_inc(sem("ybT"), 1)
            for tb, (name, n) in enumerate((("first_rows", 1), ("w_used", place[("out", 1, 1)] + 1))):
                dve.wait_ge(sem(name), n)
                x = X[:, tb * D:(tb + 1) * D]
                tt(x, x, banks(2 * tb, 2), ALU.add).then_inc(sem("x1"), 1)
            dve.wait_ge(sem("x1"), 2)
            norm(1)
            norm_evac(1, V_FFN)
            dve.wait_ge(sem("logit_ps"), 1)
            link(tt(t3(logit, 2), PS[:, 0, 256:320].rearrange("p (b e) -> p b e", b=2), bcast(bc[:, B_RT:B_RT + E], 2), ALU.add))
            for tb in range(NTB):
                lg = logit[:, tb * E:(tb + 1) * E]
                tv = top_v[:, tb * 8:(tb + 1) * 8]
                link(V.max(tv, lg))
                link(V.max_index(top_i[:, tb * 8:(tb + 1) * 8], tv, lg))
                ts(stat[:, 4 + tb:5 + tb], tv[:, 0:1], -1.0, None, ALU.mult).then_inc(sem("neg_max") if tb else sem("dve_step"), 1)
                if tb == 0:
                    count[0] += 1
            idx_f = stat[:, 104:120]
            link(V.tensor_copy(idx_f, top_i[:, :]))
            for tb in range(NTB):
                mk = MASK[:, tb * E:(tb + 1) * E]
                link(ts(mk, cc(C_EXP, E), idx_f[:, tb * 8:tb * 8 + 1], None, ALU.is_equal))
                for k in range(1, TOPK):
                    ins = stt(mk, cc(C_EXP, E), idx_f[:, tb * 8 + k:tb * 8 + k + 1], mk, ALU.is_equal, ALU.add)
                    if tb == 1 and k == TOPK - 1:
                        ins.then_inc(sem("mask"), 1)
                        dve.wait_ge(sem("mask"), 1)
                    else:
                        link(ins)
            dve.wait_ge(sem("ex"), 2)
            link(tt(EXM, EXM, MASK, ALU.mult))
            link(V.reduce_sum(stat[:, 8:10], t3(EXM, 2), AX.X))
            link(V.reciprocal(stat[:, 8:10], stat[:, 8:10]))
            g3, s3 = t3(gate_of[:, :], 2), t3(slot_of[:, :], 2)
            link(V.memset(gate_of[:, :], 0.0))
            tt(g3[:, :, 0:E], t3(EXM, 2), spread_last(stat[:, 8:10], E), ALU.mult).then_inc(sem("gates"), 1)
            dve.wait_ge(sem("pos_ps"), 1)
            link(V.memset(slot_of[:, :], -1.0))
            link(stt(s3[:, :, 0:E], PS[:, 1, 0:64].rearrange("p (b e) -> p b e", b=2), 1.0, t3(MASK, 2), ALU.add, ALU.mult))
            link(ts(s3[:, :, 0:E], s3[:, :, 0:E], 1.0, None, ALU.subtract))
            for p in range(PASSES - 1):
                link(ts(flag_f[0:1, p * E:(p + 1) * E], PS[0:1, 1, 64:96], float(CAP * (p + 1)), None, ALU.is_gt))
            link(V.reduce_max(flag_f[0:1, 96:97], flag_f[0:1, 0:E], AX.X))
            V.tensor_copy(flag_i[0:1, 0:97], flag_f[0:1, 0:97]).then_inc(sem("flags"), 1)
            dve.wait_ge(sem("flags"), 1)
            dve.wait_ge(sem("gates"), 1)

            def one_hot(e, tb, slots, weighted):
                at = bass.ds(e + tb * (E + 1), 1) if not isinstance(e, int) else slice(e + tb * (E + 1), e + tb * (E + 1) + 1)
                if weighted:
                    return ts(OHG[:, tb * P:(tb + 1) * P], slots, slot_of[:, at], gate_of[:, at], ALU.is_equal, ALU.mult)
                return ts(OH[:, tb * P:(tb + 1) * P], slots, slot_of[:, at], None, ALU.is_equal)

            def select(e):
                at = bass.ds(e + C_ID, 1) if not isinstance(e, int) else slice(C_ID + e, C_ID + e + 1)
                return V.tensor_copy(SEL, cst[0:E, at].to_broadcast([E, CAP]))

            gain_cols = spread_last(vecT[:, V_FFN:V_FFN + KC], CAP)

            def gathered_out(sig):
                tt(XG.rearrange("p (c s) -> p c s", c=KC), PS[:, 6, :].rearrange("p (c s) -> p c s", c=KC), gain_cols,
                   ALU.mult).then_inc(sem(sig), 1)

            slots0 = cc(C_SLOT)
            one_hot(0, 0, slots0, False)
            one_hot(0, 1, slots0, False).then_inc(sem("onehot"), 1)
            select(0).then_inc(sem("sel"), 1)
            dve.wait_ge(sem("gathered"), 1)
            gathered_out("x_slots")
            start = count[0]
            with dve.Fori(0, n_experts) as e:
                one_hot(e + 1, 0, slots0, False)
                one_hot(e + 1, 1, slots0, False).then_inc(sem("onehot"), 1)
                one_hot(e, 0, slots0, True)
                one_hot(e, 1, slots0, True).then_inc(sem("weighted"), 1)
                dve.wait_ge(sem("w_used"), e * PER_EXPERT + (before_experts + KC))
                ts(GLU, PS[:, 4, :], 7.0, None, ALU.min).then_inc(sem("glu"), 1)
                ts(LIN, PS[:, 5, :], 7.0, -7.0, ALU.min, ALU.max).then_inc(sem("dve_step"), 1)
                dve.wait_ge(sem("dve_step"), e * 2 + (start + 1))
                stt(LIN, LIN, 1.0, GLU, ALU.add, ALU.mult).then_inc(sem("dve_step"), 1)
                dve.wait_ge(sem("dve_step"), e * 2 + (start + 2))
                dve.wait_ge(sem("sig"), e + 1)
                tt(HH, LIN, SIG, ALU.mult).then_inc(sem("h_done"), 1)
                select(e + 1).then_inc(sem("sel"), 1)
                dve.wait_ge(sem("gathered"), e + 2)
                gathered_out("x_slots")
                dve.wait_ge(sem("w_used"), e * PER_EXPERT + (before_experts + PER_EXPERT))
                V.tensor_copy(YS, PS[:, 7, :]).then_inc(sem("y_slots"), 1)
            count[0] = start + 2 * n_experts
            any_more = dve.value_load(flag_i[0:1, 96:97])
            start = count[0]
            with dve.If(any_more > 0):
                with dve.Fori(0, PASSES - 1) as p:
                    with dve.Fori(0, E) as e:
                        more = dve.value_load(flag_i[0:1, bass.ds(p * E + e, 1)])
                        with dve.If(more > 0):
                            t = p * E + e
                            dve.wait_ge(sem("scattered"), t + n_experts)
                            slots = cst[:, bass.ds(p * P + (C_SLOT + P), P)]
                            one_hot(e, 0, slots, False)
                            one_hot(e, 1, slots, False)
                            one_hot(e, 0, slots, True)
                            one_hot(e, 1, slots, True)
                            select(e).then_inc(sem("ov_onehot"), 1)
                            dve.wait_ge(sem("ov_gathered"), t * 2 + 2)
                            gathered_out("ov_x")
                            dve.wait_ge(sem("w_used"), t * PER_EXPERT + (before_experts + KC + PER_EXPERT * E))
                            ts(GLU, PS[:, 4, :], 7.0, None, ALU.min).then_inc(sem("ov_glu"), 1)
                            ts(LIN, PS[:, 5, :], 7.0, -7.0, ALU.min, ALU.max).then_inc(sem("dve_step"), 1)
                            dve.wait_ge(sem("dve_step"), t * 2 + (start + 1))
                            stt(LIN, LIN, 1.0, GLU, ALU.add, ALU.mult).then_inc(sem("dve_step"), 1)
                            dve.wait_ge(sem("dve_step"), t * 2 + (start + 2))
                            dve.wait_ge(sem("ov_sig"), t + 1)
                            tt(HH, LIN, SIG, ALU.mult).then_inc(sem("ov_h"), 1)
                            dve.wait_ge(sem("w_used"), t * PER_EXPERT + (before_experts + PER_EXPERT * (E + 1)))
                            V.tensor_copy(YS, PS[:, 7, :]).then_inc(sem("ov_y"), 1)
                            dve.wait_ge(sem("ov_y"), t + 1)
                            dve.sem_inc(sem("pass_end"), 1)
                        with dve.Else():
                            for s in ("ov_onehot", "ov_x", "ov_glu", "ov_h", "ov_y"):
                                dve.sem_inc(sem(s), 1)
                            dve.sem_inc(sem("dve_step"), 2)
                        dve.nop()
                dve.nop()
            with dve.Else():
                dve.sem_inc(sem("dve_step"), 2 * (PASSES - 1) * E)
            count[0] = start + 2 * (PASSES - 1) * E
            dve.wait_ge(sem("scattered"), n_experts + (PASSES - 1) * E)
            for tb in range(NTB):
                x = X[:, tb * D:(tb + 1) * D]
                tt(x, x, banks(2 * tb, 2), ALU.add).then_inc(sem("x2"), 1)
            dve.wait_ge(sem("x2"), 2)
            norm(2)
            norm_evac(2, V_PLE)
            dve.wait_ge(sem("pT_high"), 1)
            low(PT[1], PS[:, 6, :], PT[0]).then_inc(sem("pT"), 1)
            dve.wait_ge(sem("ple_gate"), 1)
            for tb, (name, n) in enumerate((("first_rows", 2), ("w_used", place["ple_proj"] + 1))):
                dve.wait_ge(sem(name), n)
                x, sg = X[:, tb * D:(tb + 1) * D], SG[:, tb * D:(tb + 1) * D]
                link(tt(sg, sg, banks(4 + 2 * tb, 2), ALU.mult))
                tt(x, x, sg, ALU.add).then_inc(sem("x3"), 1)
            dve.wait_ge(sem("x3"), 2)
            link(V.memset(UB[:, :, 0:2], 0.0))
            link(V.memset(UB[:, :, 258:260], 0.0))
            norm(3)
            norm_evac(3, V_N1)

            def conv(pair):
                dve.wait_ge(sem("xbc_sb"), pair + 1)
                last = {}
                for k in range(CONVK):
                    for c in (2 * pair, 2 * pair + 1):
                        w = vecT[:, V_CW + k * CC + c:V_CW + k * CC + c + 1]
                        if k == 0:
                            ins = ts(XBT[:, c, :], UB[:, c, 0:256], w, vecT[:, V_CB + c:V_CB + c + 1], ALU.mult, ALU.add)
                        else:
                            dve.wait_ge(sem("dve_step"), last[c])
                            ins = stt(XBT[:, c, :], UB[:, c, k:k + 256], w, XBT[:, c, :], ALU.mult, ALU.add)
                        if k < CONVK - 1:
                            ins.then_inc(sem("dve_step"), 1)
                            count[0] += 1
                            last[c] = count[0]
                        else:
                            ins.then_inc(sem("conv"), 1)

            dve.wait_ge(sem("kv_sb"), 1)
            dve.wait_ge(sem("q_sb"), 1)
            qk4 = QK.rearrange("p (b h d) -> p b h d", b=2, d=HD)
            parts = []
            for tb in range(NTB):
                parts += [(qk4[:, tb, 0:8, :], gain3(B_Q2, 8)), (qk4[:, tb, 8:10, :], gain3(B_K2, 2))]
            head_squares(QK, 20, SQ2)
            link(head_scale(QK, 20, parts))
            dve.wait_ge(sem("dt_ps"), 1)
            tt(t3(DT, 2), PS[:, 6, 256:320].rearrange("p (b n) -> p b n", b=2), bcast(bc[:, B_DTB:B_DTB + 32], 2), ALU.add).then_inc(sem("dt_abs"), 1)
            for tb in range(NTB):
                for i in range(2):
                    x = qk4[:, tb, :, 32 * i:32 * i + 32]
                    at = tb * 32 + 16 * i
                    link(rotate(x[:, :, 0:16], x[:, :, 16:32], bcast(cc(C_COS + at, 16), 10), bcast(cc(C_SIN + at, 16), 10),
                                [r[:, 0:160].rearrange("p (h d) -> p h d", h=10) for r in ROT2]))
            kd = KD.rearrange("p (b h c d) -> p b h c d", b=2, h=2, c=2)
            for tb in range(NTB):
                for c in range(2):
                    ins = V.tensor_copy(kd[:, tb, :, c, :], qk4[:, tb, 8:10, :])
                    if (tb, c) != (1, 1):
                        link(ins)
            ins.then_inc(sem("qk2"), 2)
            for pair in range(3):
                conv(pair)
            dve.wait_ge(sem("dt_abs"), 1)
            dve.wait_ge(sem("a_exp"), 2)
            stt(DT, DT, 0.0, DTA, ALU.max, ALU.add).then_inc(sem("dt_sp"), 1)
            dve.wait_ge(sem("dt_sp"), 1)
            stt(t3(ADT, 2), t3(DT, 2), -1.0, bcast(AEX, 2), ALU.mult, ALU.mult).then_inc(sem("adt"), 1)
            conv(3)
            dve.wait_ge(sem("qk2T_ps"), 1)
            V.tensor_copy(QT, banks(6, 2)).then_inc(sem("qk2T"), 1)
            dve.wait_ge(sem("qk2T_ps"), 2)
            V.tensor_copy(KT, PS[:, 2, :]).then_inc(sem("qk2T"), 1)
            for u in range(4):
                dve.wait_ge(sem("s_ps"), u + 1)
                link(V.reduce_max(stat[:, 102:106], PS[:, 0:2, :].rearrange("p b (i n) -> p (b i) n", i=2), AX.X))
                ts(stat[:, 60 + 4 * u:64 + 4 * u], stat[:, 102:106], -(HD ** -0.5), None, ALU.mult).then_inc(sem("s_max"), 1)
                if u < 2:
                    conv(4 + u)
                if u == 1:
                    dve.wait_ge(sem("adt"), 1)
                    dve.wait_ge(sem("cum_ps"), 1)
                    link(V.tensor_copy(CUM, PS[:, 5, 0:64]))
                    tt(CUMX, CUM, PS[:, 5, 64:128], ALU.subtract).then_inc(sem("cum_done"), 1)
            dve.wait_ge(sem("p_exp"), 16)
            link(V.reciprocal(stat[:, 80:96], stat[:, 80:96]))
            dve.wait_ge(sem("o_ps"), 4)
            tt(heads(ATT), PS[:, 4:6, :].rearrange("p b (h d) -> p (b h) d", d=HD), spread_last(stat[:, 80:96], HD), ALU.mult).then_inc(sem("att"), 1)
            dve.wait_ge(sem("attT_high"), 1)
            low(ATTT[1], banks(4, 2), ATTT[0]).then_inc(sem("attT"), 1)
            dve.wait_ge(sem("cum_done"), 1)
            cum, cumx, dt = t3(CUM, 2), t3(CUMX, 2), t3(DT, 2)

            def exponents(h):
                dve.wait_ge(sem("abc"), h + 1)
                ps, ex = PS[:, 4 + h % 2, :], EE[h % 3]
                f, b = slice(h, h + 1), slice(16 + h, 17 + h)
                rows = ((0, 0, cum[:, 0, f]), (1, 1, cumx[:, 0, f]), (2, 1, cum[:, 1, f]),
                        (3, 2, cum[:, 0, b]), (4, 3, cum[:, 1, b]), (5, 2, cumx[:, 1, b]))
                for blk, src, by in rows:
                    ins = ts(ex[:, blk * P:(blk + 1) * P], ps[:, src * P:(src + 1) * P], by, 0.0, ALU.subtract, ALU.min)
                ins.then_inc(sem("e_sub"), 1)

            def weights(h):
                dve.wait_ge(sem("e_exp"), h + 1)
                if h >= 2:
                    dve.wait_ge(sem("y_ssd"), h - 1)
                ex, w, cbm = EE[h % 3], WW[h % 2], CBM[:, (h // 8) * 768:(h // 8 + 1) * 768]
                f, b = slice(h, h + 1), slice(16 + h, 17 + h)
                for c0, c1, by in ((0, 256, dt[:, 0, f]), (256, 384, dt[:, 1, f]), (384, 512, dt[:, 0, b]), (512, 768, dt[:, 1, b])):
                    ins = stt(w[:, c0:c1], ex[:, c0:c1], by, cbm[:, c0:c1], ALU.mult, ALU.mult)
                ins.then_inc(sem("w_ssd"), 1)
                dve.wait_ge(sem("w_ssd"), h + 1)

            g4 = GATES.rearrange("p (b n) -> p b n", b=2)
            exponents(0), exponents(1)
            dve.wait_ge(sem("cb_ps"), 1)
            for g in range(2):
                cbm = CBM[:, g * 768:(g + 1) * 768]
                ps = PS[:, 6 + g, :]
                tt(cbm[:, 0:128], ps[:, 0:128], cc(C_LE), ALU.mult)
                V.tensor_copy(cbm[:, 128:256], ps[:, 128:256])
                tt(cbm[:, 256:384], ps[:, 384:512], cc(C_LE), ALU.mult)
                tt(cbm[:, 384:512], ps[:, 0:128], cc(C_GE), ALU.mult)
                tt(cbm[:, 512:640], ps[:, 384:512], cc(C_GE), ALU.mult)
                ins = V.tensor_copy(cbm[:, 640:768], ps[:, 256:384])
            ins.then_inc(sem("cb"), 1)
            dve.wait_ge(sem("cb"), 1)
            for h in range(SSDH):
                if h + 2 < SSDH:
                    exponents(h + 2)
                weights(h)
            dve.wait_ge(sem("xs"), 1)
            dve.wait_ge(sem("z_sb"), 2)
            for tb in range(NTB):
                link(tt(Y[:, tb * D:(tb + 1) * D].rearrange("p (h d) -> p h d", d=HD),
                        XS[:, tb * D:(tb + 1) * D].rearrange("p (h d) -> p h d", d=HD),
                        spread_last(bc[:, B_DSK:B_DSK + SSDH], HD), ALU.mult))
            dve.wait_ge(sem("y_ssd"), SSDH)
            for tb in range(NTB):
                y = Y[:, tb * D:(tb + 1) * D]
                link(tt(y, y, banks(2 * tb, 2), ALU.add))
                tt(y, y, Z[:, tb * D:(tb + 1) * D], ALU.mult).then_inc(sem("y_mul"), 1)
            dve.wait_ge(sem("y_mul"), 2)
            norm(4, Y, NY)
            for g in range(2):
                dve.wait_ge(sem("w_used"), place[("attn_proj", g)] + 1)
                part = g4[:, :, g * 512:(g + 1) * 512]
                tt(part, part, PS[:, 4 + 2 * g:6 + 2 * g, :], ALU.mult).then_inc(sem("attn_out"), 1)
            dve.wait_ge(sem("attn_out"), 2)
            norm_evac(4, V_SSD)
            for tb, (name, n) in enumerate((("first_rows", 3), ("w_used", place[("ssd_proj", 1, 1)] + 1))):
                dve.wait_ge(sem(name), n)
                mix = XN[:, tb * D:(tb + 1) * D]
                link(tt(mix, banks(4 + 2 * tb, 2), g4[:, tb, D:2 * D], ALU.mult))
                tt(mix, mix, g4[:, tb, 0:D], ALU.add).then_inc(sem("mixed"), 1)
            for b in range(4):
                dve.wait_ge(sem("mixT_high"), b + 1)
                cols = slice(b * 512, (b + 1) * 512)
                low(XNT[1][:, cols], PS[:, b, :], XNT[0][:, cols]).then_inc(sem("mixT"), 1)

            def post_norm(i, gain, signal):
                for tb in range(NTB):
                    dve.wait_ge(sem("post_sd"), 2 * i + tb + 1)
                    link(V.reciprocal(stat[:, 6 + tb:7 + tb], stat[:, 2 + tb:3 + tb]))
                    half = XN[:, tb * D:(tb + 1) * D]
                    link(stt(half, banks(2 * tb, 2), stat[:, 6 + tb:7 + tb], gain, ALU.mult, ALU.mult))
                    x = X[:, tb * D:(tb + 1) * D]
                    tt(x, x, half, ALU.add).then_inc(sem(signal), 1)

            dve.wait_ge(sem("post1_in"), 16)
            post_norm(0, N1P, "x4")
            dve.wait_ge(sem("x4"), 2)
            norm(5)
            norm_evac(5, V_N2)
            for j in range(FC // 2):
                dve.wait_ge(sem("w_used"), place[("up", j)] + 1)
                dve.wait_ge(sem("silu_f"), j + 1)
                cols, prod = slice(j * 512, (j + 1) * 512), PROD[j % 2]
                link(tt(prod, SF[j % 2], PS[:, 2 * (j % 4) + 1, :], ALU.mult))
                link(V.tensor_copy(ACTT[0][:, cols], prod))
                low(ACTT[1][:, cols], prod, ACTT[0][:, cols]).then_inc(sem("ffn_act"), 1)
            dve.wait_ge(sem("post2_in"), 16)
            post_norm(1, N2P, "done")

        @block.gpsimd
        def _(pool):
            for m, key in enumerate(keys):
                pool.wait_ge(sem("w_high"), m + 1)
                n = size(key)
                nc.gpsimd.tensor_tensor(LOW[m % BUF][:, 0:n], slot(raw_slot(key))[:, 0:n], HIGH[m % BUF][:, 0:n].bitcast(F32),
                                        ALU.subtract).then_inc(sem("w_low"), 1)


_INS = ["x", "p", "positions", "g_mix_norm", "w_in", "sb_q_gain", "sb_k_gain", "ret_q_gain", "ret_k_gain",
        "ret_gn_gain", "ret_gn_bias", "w_out", "g_ffn_norm", "w_router", "b_router", "w_up_gate", "b_up_gate",
        "w_down", "b_down", "g_ple_norm", "w_ple_gate", "w_ple_proj", "w_in_2", "q_norm_2", "k_norm_2", "conv_w_2",
        "conv_b_2", "dt_bias_f_2", "dt_bias_b_2", "a_log_f_2", "a_log_b_2", "d_skip_2", "ssd_norm_2",
        "w_attn_proj_2", "w_ssd_proj_2", "w_out_2", "norm1_pre_2", "norm1_post_2", "norm2_pre_2", "norm2_post_2",
        "w_gate_up_2", "w_down_2"]


def kernel(**inputs):
    import concourse.bacc as _bacc
    from concourse.bass_utils import run_bass_kernel_spmd as _run

    nc = _bacc.Bacc("TRN2", target_bir_lowering=False, num_devices=1)
    arrays, aps = {}, {}
    for name in _INS:
        arr = np.ascontiguousarray(inputs[name])
        arrays[f"in_{name}"] = arr
        aps[name] = nc.dram_tensor(f"in_{name}", arr.shape, mybir.dt.from_np(arr.dtype), kind="ExternalInput").ap()
    arrays["consts"] = constants()
    aps["consts"] = nc.dram_tensor("consts", (P, NCONST), F32, kind="ExternalInput").ap()
    out = nc.dram_tensor("out", (1, T, D), F32, kind="ExternalOutput").ap()
    build_program(nc, aps, out)
    r = _run(nc, [arrays], core_ids=[0])
    return r.results[0]["out"]
```
